# Optimizing a Trainium2 kernel written in Bass

```python
import math, functools
import jax, jax.numpy as jnp
from jax import lax
import numpy as np

D_MODEL = 1024
BATCH = 1
SEQ = 1024
DEPTH = 1
DEC_BATCH = 8
DEC_SEQ = 4
PAST_LEN = 256
PAGE_SIZE = 128

GLA_HEADS = 4
GLA_DK = D_MODEL // 2
GLA_DV = D_MODEL
GLA_HEAD_DK = GLA_DK // GLA_HEADS
GLA_HEAD_DV = GLA_DV // GLA_HEADS
GLA_GATE_RANK = 16
GLA_GATE_TAU = 16.0
GLA_CHUNK = 64
DSA_HEADS = 8
DSA_HEAD_DIM = 64
DSA_WIDTH = DSA_HEADS * DSA_HEAD_DIM
IDX_HEADS = 4
IDX_DIM = 64
TOPK_MAX = 256
QUERY_BLOCK = 128
REL_BUCKETS = 32
REL_MAX_DIST = 128
D_FF = ((8 * D_MODEL + 3 * 256 - 1) // (3 * 256)) * 256
RMS_EPS = 1e-6
LN_EPS = 1e-6
SPLIT_SIZES = (GLA_DK, GLA_DK, GLA_DV, GLA_DV, GLA_GATE_RANK,
               DSA_WIDTH, DSA_WIDTH, DSA_WIDTH, IDX_HEADS * IDX_DIM, IDX_DIM, IDX_HEADS,
               D_MODEL, D_MODEL)
D_IN_PROJ = sum(SPLIT_SIZES)

kernel_name = "gla_dsa_gated_hybrid_step"

def _rmsnorm(x, g):
    xf = x.astype(jnp.float32)
    y = xf * lax.rsqrt(jnp.mean(xf * xf, axis=-1, keepdims=True) + RMS_EPS)
    return (y * g.astype(jnp.float32)).astype(x.dtype)

def _layernorm(x, g, b):
    xf = x.astype(jnp.float32)
    mu = jnp.mean(xf, axis=-1, keepdims=True)
    var = jnp.mean(jnp.square(xf - mu), axis=-1, keepdims=True)
    y = (xf - mu) * lax.rsqrt(var + LN_EPS) * g.astype(jnp.float32) + b.astype(jnp.float32)
    return y.astype(x.dtype)

def _project(h, w_in, w_gate_up, b_gate, idx_k_g, idx_k_b):
    B, L, _ = h.shape
    z = h @ w_in
    points = [int(p) for p in np.cumsum(SPLIT_SIZES)[:-1]]
    (q_g, k_g, v_g, r_g, a_low, q_d, k_d, v_d, q_i, k_i, w_i, gate_g, gate_d) = jnp.split(z, points, axis=-1)
    log_a = jax.nn.log_sigmoid((a_low @ w_gate_up + b_gate).astype(jnp.float32)) / GLA_GATE_TAU
    heads = lambda a, n: a.reshape(B, L, n, -1)
    return (heads(q_g, GLA_HEADS), heads(k_g, GLA_HEADS), heads(v_g, GLA_HEADS), r_g,
            heads(log_a, GLA_HEADS),
            heads(q_d, DSA_HEADS), heads(k_d, DSA_HEADS), heads(v_d, DSA_HEADS),
            heads(q_i, IDX_HEADS), _layernorm(k_i, idx_k_g, idx_k_b), w_i, gate_g, gate_d)

def _gla_chunked(q, k, v, log_a, s0):
    B, L, H, _ = q.shape
    C = math.gcd(L, GLA_CHUNK)
    n = L // C

    def chunks(a):
        return jnp.moveaxis(a.astype(jnp.float32).reshape(B, n, C, *a.shape[2:]), 1, 0)

    causal = jnp.tril(jnp.ones((C, C), dtype=bool))[None, :, :, None, None]

    def step(S, inp):
        qc, kc, vc, gc = inp
        b = jnp.cumsum(gc, axis=1)
        diff = jnp.where(causal, b[:, :, None] - b[:, None, :], -jnp.inf)
        att = jnp.einsum('bthd,bshd,btshd->btsh', qc, kc, jnp.exp(diff))
        o = (jnp.einsum('btsh,bshv->bthv', att, vc)
             + jnp.einsum('bthd,bhdv->bthv', qc * jnp.exp(b), S))
        b_last = b[:, -1]
        S = (S * jnp.exp(b_last)[..., None]
             + jnp.einsum('bshd,bshv->bhdv', kc * jnp.exp(b_last[:, None] - b), vc))
        return S, o

    S, o = lax.scan(step, s0.astype(jnp.float32),
                    (chunks(q * (GLA_HEAD_DK ** -0.5)), chunks(k), chunks(v), chunks(log_a)))
    o = jnp.moveaxis(o, 0, 1).reshape(B, L, H, -1)
    return o, S

def _t5_bucket(rel):
    max_exact = REL_BUCKETS // 2
    n = jnp.maximum(rel, 0)
    large = max_exact + (jnp.log(jnp.maximum(n, 1).astype(jnp.float32) / max_exact)
                         / math.log(REL_MAX_DIST / max_exact)
                         * (REL_BUCKETS - max_exact)).astype(jnp.int32)
    large = jnp.minimum(large, REL_BUCKETS - 1)
    return jnp.where(n < max_exact, n, large)

def _indexer_topk(q_i, w_i, k_i, t_pos, topk):
    s = jnp.einsum('bqhd,bsd->bqhs', q_i.astype(jnp.float32), k_i.astype(jnp.float32)) * (IDX_DIM ** -0.5)
    score = jnp.einsum('bqhs,bqh->bqs', jax.nn.relu(s), w_i.astype(jnp.float32) * (IDX_HEADS ** -0.5))
    key_pos = jnp.arange(k_i.shape[1])
    score = jnp.where(key_pos[None, None, :] <= t_pos[None, :, None], score, -jnp.inf)
    _, idx = lax.top_k(score, topk)
    return idx

def _sparse_attend(q, k_sel, v_sel, idx, t_pos, rel_bias):
    rel = t_pos[None, :, None] - idx
    bias = jnp.swapaxes(rel_bias.astype(jnp.float32)[_t5_bucket(rel)], -1, -2)
    logits = jnp.einsum('bqhd,bqkhd->bqhk', q.astype(jnp.float32), k_sel.astype(jnp.float32)) * (DSA_HEAD_DIM ** -0.5) + bias
    logits = jnp.where(rel[:, :, None, :] >= 0, logits, -jnp.inf)
    p = jax.nn.softmax(logits, axis=-1)
    return jnp.einsum('bqhk,bqkhd->bqhd', p, v_sel.astype(jnp.float32)).astype(q.dtype)

def _gather_rows(rows, ix):
    return jax.vmap(lambda r, i: r[i])(rows, ix)

def _dsa_prompt(q, k, v, q_i, w_i, k_i, rel_bias):
    B, L = q.shape[:2]
    topk = min(TOPK_MAX, L // 4)
    nb = L // QUERY_BLOCK

    def blocks(a):
        return jnp.moveaxis(a.reshape(B, nb, QUERY_BLOCK, *a.shape[2:]), 1, 0)

    def one_block(inp):
        blk, qb, qib, wib = inp
        t_pos = blk * QUERY_BLOCK + jnp.arange(QUERY_BLOCK)
        idx = _indexer_topk(qib, wib, k_i, t_pos, topk)
        return _sparse_attend(qb, _gather_rows(k, idx), _gather_rows(v, idx), idx, t_pos, rel_bias)

    out = lax.map(one_block, (jnp.arange(nb), blocks(q), blocks(q_i), blocks(w_i)))
    return jnp.moveaxis(out, 0, 1).reshape(B, L, DSA_HEADS, DSA_HEAD_DIM)

def _dsa_sample(q, k_new, v_new, q_i, w_i, k_i_new, rel_bias, cache_k, cache_v, cache_kidx, page_table):
    DB, T = q.shape[:2]
    past = page_table.shape[1] * PAGE_SIZE
    topk = min(TOPK_MAX, (past + T) // 4)
    t_pos = past + jnp.arange(T)
    k_i_past = cache_kidx[page_table].reshape(DB, past, IDX_DIM)
    k_i_all = jnp.concatenate([k_i_past, k_i_new.astype(k_i_past.dtype)], axis=1)
    idx = _indexer_topk(q_i, w_i, k_i_all, t_pos, topk)
    in_past = (idx < past)[..., None, None]
    pidx = jnp.minimum(idx, past - 1)
    phys = _gather_rows(page_table, pidx // PAGE_SIZE)
    slot = pidx % PAGE_SIZE
    nidx = jnp.clip(idx - past, 0, T - 1)
    k_sel = jnp.where(in_past, cache_k[phys, slot], _gather_rows(k_new, nidx).astype(cache_k.dtype))
    v_sel = jnp.where(in_past, cache_v[phys, slot], _gather_rows(v_new, nidx).astype(cache_v.dtype))
    return _sparse_attend(q, k_sel, v_sel, idx, t_pos, rel_bias)

def _trunk_layer(x, gla_s0, dsa_fn, rel_bias, lw):
    (g_mix, w_in, w_gate_up, b_gate, gla_norm_g, w_gla_branch, idx_k_g, idx_k_b,
     w_dsa_branch, w_o, g_ffn, w_ffn_gate, w_ffn_up, w_ffn_down) = lw
    B, L, _ = x.shape
    h = _rmsnorm(x, g_mix)
    (q_g, k_g, v_g, r_g, log_a, q_d, k_d, v_d, q_i, k_i, w_i, gate_g, gate_d) = _project(
        h, w_in, w_gate_up, b_gate, idx_k_g, idx_k_b)
    o_g, s_new = _gla_chunked(q_g, k_g, v_g, log_a, gla_s0)
    o_g = _rmsnorm(o_g.astype(x.dtype), gla_norm_g).reshape(B, L, GLA_DV) * jax.nn.silu(r_g)
    y_g = o_g @ w_gla_branch
    o_d = dsa_fn(q_d, k_d, v_d, q_i, w_i, k_i, rel_bias)
    y_d = o_d.reshape(B, L, DSA_WIDTH) @ w_dsa_branch
    x = x + (jax.nn.sigmoid(gate_g) * y_g + jax.nn.sigmoid(gate_d) * y_d) @ w_o
    hf = _rmsnorm(x, g_ffn)
    x = x + (jax.nn.silu(hf @ w_ffn_gate) * (hf @ w_ffn_up)) @ w_ffn_down
    return x, (k_d, v_d, k_i, s_new.astype(gla_s0.dtype))

def setup_inputs(seed: int = 0) -> dict:
    key = jax.random.key(seed)
    ks = jax.random.split(key, 32)
    n_pages = PAST_LEN // PAGE_SIZE
    n_used = DEC_BATCH * n_pages
    n_pool = n_used + n_used // 4

    def nrm(k, shape, scale):
        return jax.random.normal(k, shape, jnp.float32) * scale

    def gain(k, shape):
        return 1.0 + nrm(k, shape, 0.05)

    page_table = jax.random.permutation(ks[7], n_pool)[:n_used].reshape(DEC_BATCH, n_pages).astype(jnp.int32)
    return {
        "x_prompt": nrm(ks[0], (BATCH, SEQ, D_MODEL), 1.0),
        "x_sample": nrm(ks[1], (DEC_BATCH, DEC_SEQ, D_MODEL), 1.0),
        "cache_k": nrm(ks[2], (DEPTH, n_pool, PAGE_SIZE, DSA_HEADS, DSA_HEAD_DIM), 1.0),
        "cache_v": nrm(ks[3], (DEPTH, n_pool, PAGE_SIZE, DSA_HEADS, DSA_HEAD_DIM), 1.0),
        "cache_kidx": nrm(ks[4], (DEPTH, n_pool, PAGE_SIZE, IDX_DIM), 1.0),
        "state_gla": nrm(ks[5], (DEPTH, DEC_BATCH, GLA_HEADS, GLA_HEAD_DK, GLA_HEAD_DV), 0.3),
        "page_table": page_table,
        "g_mix": gain(ks[8], (DEPTH, D_MODEL)),
        "w_in": nrm(ks[9], (DEPTH, D_MODEL, D_IN_PROJ), D_MODEL ** -0.5),
        "w_gate_up": nrm(ks[10], (DEPTH, GLA_GATE_RANK, GLA_DK), GLA_GATE_RANK ** -0.5),
        "b_gate": nrm(ks[11], (DEPTH, GLA_DK), 0.1),
        "gla_norm_g": gain(ks[12], (DEPTH, GLA_HEAD_DV)),
        "w_gla_branch": nrm(ks[13], (DEPTH, GLA_DV, D_MODEL), GLA_DV ** -0.5),
        "idx_k_g": gain(ks[14], (DEPTH, IDX_DIM)),
        "idx_k_b": nrm(ks[15], (DEPTH, IDX_DIM), 0.02),
        "w_dsa_branch": nrm(ks[16], (DEPTH, DSA_WIDTH, D_MODEL), DSA_WIDTH ** -0.5),
        "w_o": nrm(ks[17], (DEPTH, D_MODEL, D_MODEL), D_MODEL ** -0.5),
        "g_ffn": gain(ks[18], (DEPTH, D_MODEL)),
        "w_ffn_gate": nrm(ks[19], (DEPTH, D_MODEL, D_FF), D_MODEL ** -0.5),
        "w_ffn_up": nrm(ks[20], (DEPTH, D_MODEL, D_FF), D_MODEL ** -0.5),
        "w_ffn_down": nrm(ks[21], (DEPTH, D_FF, D_MODEL), D_FF ** -0.5),
        "rel_bias": nrm(ks[22], (REL_BUCKETS, DSA_HEADS), 0.5),
        "g_final": gain(ks[23], (D_MODEL,)),
    }

def reference(x_prompt, x_sample, cache_k, cache_v, cache_kidx, state_gla, page_table,
              g_mix, w_in, w_gate_up, b_gate, gla_norm_g, w_gla_branch, idx_k_g, idx_k_b,
              w_dsa_branch, w_o, g_ffn, w_ffn_gate, w_ffn_up, w_ffn_down, rel_bias, g_final):
    xp, xs = x_prompt, x_sample
    new_p = ([], [], [], [])
    new_s = ([], [], [], [])
    for layer in range(DEPTH):
        lw = (g_mix[layer], w_in[layer], w_gate_up[layer], b_gate[layer], gla_norm_g[layer],
              w_gla_branch[layer], idx_k_g[layer], idx_k_b[layer], w_dsa_branch[layer], w_o[layer],
              g_ffn[layer], w_ffn_gate[layer], w_ffn_up[layer], w_ffn_down[layer])
        s0 = jnp.zeros((xp.shape[0], GLA_HEADS, GLA_HEAD_DK, GLA_HEAD_DV), state_gla.dtype)
        xp, st_p = _trunk_layer(xp, s0, _dsa_prompt, rel_bias, lw)
        dsa_s = functools.partial(_dsa_sample, cache_k=cache_k[layer], cache_v=cache_v[layer],
                                  cache_kidx=cache_kidx[layer], page_table=page_table)
        xs, st_s = _trunk_layer(xs, state_gla[layer], dsa_s, rel_bias, lw)
        for lst, a in zip(new_p, st_p):
            lst.append(a)
        for lst, a in zip(new_s, st_s):
            lst.append(a)
    y_prompt = _rmsnorm(xp, g_final)
    y_sample = _rmsnorm(xs, g_final)
    k_p, v_p, ki_p, s_p = [jnp.stack(a) for a in new_p]
    k_s, v_s, ki_s, s_s = [jnp.stack(a) for a in new_s]
    return (y_prompt, y_sample, k_p, v_p, ki_p, s_p, k_s, v_s, ki_s, s_s)


_drawn_inputs = setup_inputs


def setup_inputs(seed=0):
    import zlib

    import numpy as np

    out = dict(_drawn_inputs(seed))
    spreads = {}
    factors = {'gla_norm_g': 3.445, 'idx_k_b': 3.041}
    for name, (base, spread) in spreads.items():
        noise = np.random.default_rng([zlib.crc32(name.encode()), seed]).standard_normal(out[name].shape)
        drawn = base * np.exp(spread * noise) if base else spread * noise
        out[name] = __import__('jax').numpy.asarray(drawn.astype(out[name].dtype))
    for name, factor in factors.items():
        out[name] = (out[name] * factor).astype(out[name].dtype)
    return out
```

```python
from contextlib import ExitStack

import numpy as np

import concourse.bass as bass
from concourse import mybir

F32 = mybir.dt.float32
I32 = mybir.dt.int32
ALU = mybir.AluOpType
ACT = mybir.ActivationFunctionType
X = mybir.AxisListType.X

P = 128
D = 1024
SEQ = 1024
DB, DT = 8, 4
NS = DB * DT
T = SEQ + NS
NTP = SEQ // P
NT = NTP + 1
KD = D // P
PAST, PAGE = 256, 128
NPG = PAST // PAGE
NKS = PAST + DT
GH, GDK, GDV = 4, 128, 256
RANK = 16
DH, DHD = 8, 64
DW = DH * DHD
IH, IDM = 4, 64
TOPK = 256
TOPK_S = NKS // 4
DFF = 2816
KF = DFF // P
NB = 32
EPS = 1e-6
NEG = -1e30
SPLITS = dict(qg=512, kg=512, vg=1024, rg=1024, al=RANK, qd=DW, kd=DW, vd=DW, qi=IH * IDM,
              ki=IDM, wi=IH, gg=D, gd=D)
COL, _at = {}, 0
for _name, _w in SPLITS.items():
    COL[_name] = _at
    _at += _w
DIN = _at
W3 = T // 3
TCH = [(n * W3, W3) for n in range(3)]
OHW = 387


def rows(i):
    return P if i < NTP else NS


def constants():
    r = np.arange(P)
    j, q = r // 32, r % 32
    h, t = q // 4, q % 4
    tok_b, tok_t = np.arange(NS) // DT, np.arange(NS) % DT
    own = lambda g: (tok_b[:, None] == 4 * g + j[None]) & (tok_t[:, None] == t[None])
    exp_i = np.stack([own(g) & (h < IH)[None] for g in range(2)], 1)
    exp_h = np.stack([own(g) for g in range(2)], 1)
    n = np.maximum(259 - np.arange(OHW), 0)
    half = NB // 2
    large = half + (np.log(np.maximum(n, 1).astype(np.float32) / np.float32(half))
                    / np.float32(np.log(128 / half)) * np.float32(NB - half)).astype(np.int32)
    bucket = np.where(n < half, n, np.minimum(large, NB - 1))
    onehot = np.arange(NB)[:, None] == bucket[None]
    f = lambda a: np.ascontiguousarray(np.asarray(a, np.float32).reshape(a.shape[0], -1))
    s, c = np.arange(P), np.arange(P)
    c128 = {
        "ident": f(np.eye(P)),
        "causal": f(c[None] >= s[:, None]),
        "sum_i": f(np.transpose(exp_i, (2, 1, 0))),
        "pick_i": f((h[:, None] == np.arange(IH)[None])),
        "pick_h": f((h[:, None] == np.arange(DH)[None])),
        "pick_b": f(np.stack([(4 * g + j)[:, None] == np.arange(DB)[None] for g in range(2)], 1)),
        "sum_t": f((j[:, None] == np.arange(16)[None] // 4) & (t[:, None] == np.arange(16)[None] % 4)),
        "cols_b": f(np.broadcast_to(np.arange(NS)[None, None] // DT == np.arange(DB)[None, :, None],
                                    (P, DB, NS))),
        "bits_f": f(np.broadcast_to(np.append(2.0 ** np.arange(30, -1, -1), 0.0), (P, 32))),
    }
    future = tok_t[:, None] < np.arange(DT)[None]
    c32 = {
        "exp_i": f(exp_i), "exp_h": f(exp_h), "onehot": f(onehot),
        "same": f((tok_b[:, None] == tok_b[None]) & (tok_t[:, None] <= tok_t[None])),
        "future": f(np.where(future, NEG, 0.0)),
        "rows_b": f(tok_b[:, None] == np.arange(DB)[None]),
    }
    bits = np.broadcast_to(np.append(1 << np.arange(30, -1, -1), 0).astype(np.int32), (P, 32))
    return c128, c32, np.ascontiguousarray(bits)


def widths(table):
    out, at = {}, 0
    for k, v in table.items():
        out[k] = (at, v.shape[1])
        at += v.shape[1]
    return out, at


def build(nc, a, o, c128_at, c32_at):
    ctx = ExitStack()
    with ctx:
        sem = lambda n: ctx.enter_context(nc.semaphore(n))
        n128, n32 = sum(w for _, w in c128_at.values()), sum(w for _, w in c32_at.values())

        ARENA = 53200
        arena = ctx.enter_context(nc.sbuf_tensor("arena", [P, ARENA], F32))
        top = [0]

        def region(n):
            at = top[0]
            top[0] += n
            assert top[0] <= ARENA, top[0]
            return at

        def at(off, *shape):
            n = int(np.prod(shape))
            v = arena[:, off:off + n]
            if len(shape) == 2:
                v = v.rearrange("p (a b) -> p a b", a=shape[0])
            if len(shape) == 3:
                v = v.rearrange("p (a b c) -> p a b c", a=shape[0], b=shape[1])
            return v

        o_c128, o_c32 = region(n128), region(n32)
        k128 = {k: arena[:, o_c128 + s:o_c128 + s + w] for k, (s, w) in c128_at.items()}
        k32 = {k: arena[0:32, o_c32 + s:o_c32 + s + w] for k, (s, w) in c32_at.items()}
        ident = k128["ident"]
        small = region(420)
        o_hT = region(KD * T)
        o_w = region(2 * 4096)
        base = top[0]

        hT = at(o_hT, KD, T)
        wslot = [arena[:, o_w + s * 4096:o_w + (s + 1) * 4096] for s in range(2)]

        s_at = [small]

        def tiny(n, dt=F32):
            v = arena[:, s_at[0]:s_at[0] + n]
            s_at[0] += n
            assert s_at[0] <= small + 420
            return v if dt == F32 else v.bitcast(dt)

        vec = tiny(22)
        ssq, msq, rt, rstd = tiny(NT), tiny(NT), tiny(NT), tiny(NT)
        one = tiny(1)
        kmu, kvar, krt, krs = tiny(NT), tiny(NT), tiny(NT), tiny(NT)
        cnt, need = tiny(7), tiny(7)
        thr, gbit = tiny(7, I32), tiny(7, I32)
        cand = tiny(7, I32)
        bits = tiny(32, I32)
        wrow = tiny(2)
        wtmp = tiny(4)
        mxa, mxb, nmx, rsum, rrec = tiny(4), tiny(4), tiny(4), tiny(4), tiny(4)
        ebl = tiny(NTP + DB)
        relb = tiny(DH)
        r31 = tiny(DH)
        pagetab = tiny(16, I32)
        oss, oms, ort, ors = tiny(NT), tiny(NT), tiny(NT), tiny(NT)

        ring = ctx.enter_context(nc.psum_tensor("ring", [P, 4, 512], F32))
        lgt = [ctx.enter_context(nc.psum_tensor(f"lgt{i}", [P, 1024], F32)) for i in range(2)]
        full = [sem(f"full{i}") for i in range(4)]
        evac = [sem(f"evac{i}") for i in range(4)]
        ready = [0]
        chunk = {}

        def plan(*key):
            chunk[key] = ready[0]
            ready[0] += 1

        plan("vec")
        for i in range(NT):
            plan("h", i, 0), plan("h", i, 1)
        for h in range(DH):
            plan("nb", h)
        for f in range(2):
            for n in range(3):
                plan("qi", f, n)
        for i in range(NT):
            plan("ki", i)
        for n in range(3):
            plan("al", n)
        for n in range(3):
            plan("kiT", n)
        for n in range(4):
            plan("ps", n)
        SCC = [(b, h, c0, min(512, P * (b + 1) - c0)) for b in range(2, NTP)
               for c0 in range(0, P * (b + 1), 512) for h in range(IH)]
        for k in SCC:
            plan("sc", *k)
        for g in range(2):
            plan("wr", g), plan("si", g)
        plan("ss")
        for w in ("qd", "kd"):
            for f in range(4):
                for n in range(3):
                    plan(w, f, n)
        for i in range(NT):
            plan("kt", i)
        for i in range(NT):
            plan("vd", i)
        UN = [(b, h) for b in range(NTP) for h in range(DH)]
        for u in range(len(UN) + 1):
            if u >= 1:
                plan("o", u - 1)
                if u % DH == 0:
                    plan("ot", u // DH - 1)
            if u < len(UN):
                for c in range((UN[u][0] + 4) // 4):
                    plan("pt", u, c)
        for g in range(2):
            for j in range(4):
                for p in range(NPG):
                    plan("kp", g, j, p)
            plan("mb", g)
        for g in range(2):
            plan("sl", g), plan("spt", g), plan("so", g), plan("sot", g)
        for h in range(GH):
            for w in ("gq", "gk"):
                for n in range(3):
                    plan(w, h, n)
            if h >= 1:
                for i in range(NT):
                    plan("gt", h - 1, i)
            for n in range(3):
                plan("gz", h, n)
            for i in range(NT):
                plan("gv", h, i)
            for f in range(2):
                for n in range(3):
                    plan("gr", h, f, n)
            plan("at", h, 0), plan("k4", h, 0)
            for i in range(NTP):
                plan("at", h, i + 1), plan("k4", h, i + 1)
                plan("go", h, i), plan("ds", h, i)
            plan("go", h, NTP)
            for b in range(DB):
                plan("ds", h, NTP + b)
        for i in range(NT):
            plan("gt", GH - 1, i)
        for f in range(KD):
            for n in range(3):
                for w in ("mg", "my", "me", "mz"):
                    plan(w, f, n)
        for i in range(NT):
            plan("wo", i, 0), plan("wo", i, 1)
            if i >= 2:
                plan("h2", i - 2, 0), plan("h2", i - 2, 1)
        for i in (NT - 2, NT - 1):
            plan("h2", i, 0), plan("h2", i, 1)
        for f in range(KF):
            for n in range(3):
                plan("fg", f, n), plan("fu", f, n)
        for f in range(KD):
            for n in range(3):
                plan("dn", f, n)
        for i in range(NT):
            plan("yt", i, 0), plan("yt", i, 1)

        def bank(*key):
            return ring[:, chunk[key] % 4, :]

        def wait_full(eng, *key):
            eng.wait_ge(full[chunk[key] % 4], chunk[key] // 4 + 1)

        def wait_evac(eng, *key):
            eng.wait_ge(evac[chunk[key] % 4], chunk[key] // 4 + 1)

        def evacuates(ins, *key):
            return ins.then_inc(evac[chunk[key] % 4], 1)

        def wsrc(name, c0, n, k=KD):
            return a[name].rearrange("l (k p) n -> p (l k) n", p=P)[:, 0:k, c0:c0 + n]

        units = [("idx", [("w_in", COL["qi"], 324, 0), ("w_in", COL["al"], RANK, 324)], 340, KD)]
        for w in ("qd", "kd", "vd"):
            units.append((w, [("w_in", COL[w], 512, 0)], 512, KD))
        for h in range(GH):
            units.append((("qkv", h), [("w_in", COL["qg"] + GDK * h, GDK, 0),
                                       ("w_in", COL["kg"] + GDK * h, GDK, GDK),
                                       ("w_in", COL["vg"] + GDV * h, GDV, 2 * GDK)], 512, KD))
            units.append((("r", h), [("w_in", COL["rg"] + GDV * h, GDV, 0)], GDV, KD))
        for f in range(KD):
            units.append((("m", f), None, 0, 0))
        for s in range(2):
            units.append((("wo", s), [("w_o", 512 * s, 512, 0)], 512, KD))
        for f in range(KF // 2):
            units.append((("ff", f), [("w_ffn_gate", 256 * f, 256, 0), ("w_ffn_up", 256 * f, 256, 256)],
                          512, KD))
        for f in range(KD):
            units.append((("dn", f), [("w_ffn_down", P * f, P, 0)], P, KF))
        unit_no = {u[0]: n for n, u in enumerate(units)}
        w_landed = [sem(f"w_landed{s}") for s in range(2)]
        last_chunk = {"idx": ("al", 2), "qd": ("qd", 3, 2), "kd": ("kd", 3, 2), "vd": ("vd", NTP),
                      ("wo", 0): ("wo", NTP, 0), ("wo", 1): ("wo", NTP, 1)}
        for h in range(GH):
            last_chunk["qkv", h], last_chunk["r", h] = ("gv", h, NTP), ("gr", h, 1, 2)
        for f in range(KD):
            last_chunk["m", f], last_chunk["dn", f] = ("mz", f, 2), ("dn", f, 2)
        for f in range(KF // 2):
            last_chunk["ff", f] = ("fu", 2 * f + 1, 2)
        w_count = []
        per = [0, 0]
        for n, (_, parts, _, _) in enumerate(units):
            per[n % 2] += 4 if parts is None else len(parts)
            w_count.append(16 * per[n % 2])

        def wview(name):
            n = unit_no[name]
            _, parts, w, k = units[n]
            if parts is None:
                return wslot[n % 2][:, 0:28 * P].rearrange("p (k n) -> p k n", n=P)
            return wslot[n % 2][:, 0:k * w].rearrange("p (k n) -> p k n", n=w)

        def wait_w(eng, name):
            n = unit_no[name]
            eng.wait_ge(w_landed[n % 2], w_count[n])

        o_attn = base
        top[0] = base
        o_SC = region(4484)
        o_alT = region(T)
        o_odT = region(4 * T)
        o_tail = top[0]
        SCAT, _n = {}, 0
        for b in range(2, NTP):
            SCAT[b] = _n
            _n += P * (b + 1)
        SC = arena[:, o_SC:o_SC + 4484]
        scs = SC[:, _n:_n + NKS]
        alT = at(o_alT, T)
        odT = at(o_odT, 4, T)
        o_qd = region(4 * T)
        o_kd = region(4 * T)
        o_vd = region(NT * DW)
        o_nb = region(DH * 256)
        o_free = top[0]
        qdT, kdT, vd = at(o_qd, 4, T), at(o_kd, 4, T), at(o_vd, NT, DW)
        nearb = at(o_nb, DH, 256)
        xa = [arena[:, o_qd + i * D:o_qd + (i + 1) * D] for i in range(4)]
        sqj = arena[:, o_kd:o_kd + D]
        relx = at(o_kd + D, DH, P)
        top[0] = o_free
        kw = at(region(NT * 68), NT, 68)
        kn = at(region(NT * P), NT, P)
        kd2 = at(region(NT * IDM), NT, IDM)
        kiT = at(region(T), T)
        qiT = at(region(2 * T), 2, T)
        o_gb = region(2 * IDM)
        kg_b, kb_b = at(o_gb, IDM), at(o_gb + IDM, IDM)
        assert top[0] <= ARENA
        kiS = at(o_odT, DB, PAST)
        qiS = at(o_odT + DB * PAST, DB * 2, 32)
        rl = [arena[:, o_odT + 2560 + i * 512:o_odT + 2560 + (i + 1) * 512] for i in range(2)]
        rs_s = arena[:, o_odT + 3584:o_odT + 3584 + NKS]
        kpg = at(o_vd, 16, P)
        nbs = [arena[:, o_vd + 2048 + i * 384:o_vd + 2048 + i * 384 + 383] for i in range(2)]
        vrow = arena[:, o_vd + 2048 + 768:o_vd + 2048 + 768 + P]
        top[0] = o_free
        nlg = [at(region(1024), 1024) for _ in range(2)]
        pr = [at(region(1024), 1024) for _ in range(2)]
        junk = at(o_free + NT * (68 + P + IDM), 1121).bitcast(mybir.dt.uint8)
        top[0] = o_free + NT * 68 + NT * P + NT * IDM + T + 2 * T + 2 * IDM
        kst = [at(region(DW), DW) for _ in range(2)]
        print("selection top", top[0])
        top[0] = o_free
        nlg = [at(region(1024), 1024) for _ in range(2)]
        pr = [at(region(1024), 1024) for _ in range(2)]
        pT = [at(region(1024), 8, P) for _ in range(2)]
        nearm = [at(region(256), 256) for _ in range(4)]
        osb = [at(region(DW), DW) for _ in range(2)]
        nearz = at(region(256), 256)
        U16 = mybir.dt.uint16
        eqc, inc = at(region(512), 512).bitcast(U16), at(region(512), 512).bitcast(U16)
        print("attention top", top[0])
        kpS = [at(o_SC + i * NPG * DW, NPG, DW) for i in range(2)]
        top[0] = o_free
        vpS = [at(region(NPG * DW), NPG, DW) for _ in range(4)]
        kTs = [at(region(4 * PAST), 4, PAST) for _ in range(2)]
        mbS = [at(region(NKS), NKS) for _ in range(2)]
        nlS = [at(region(NKS), NKS) for _ in range(2)]
        prS = [at(region(NKS), NKS) for _ in range(2)]
        pnS = at(region(NS), DB, DT)
        ptS = at(region(3 * P), 3, P)
        omS = at(region(DW), DW)
        assert top[0] <= ARENA, top[0]
        qbS = at(o_nb, DB * 4, 32)
        relt = at(o_nb + 1024, 4, P)

        top[0] = base
        o_SC2 = region(4484)
        region(T)
        region(4 * T)
        ogT = at(region(KD * T), KD, T)
        qh, kh = at(region(T), T), at(region(T), T)
        Bc = at(region(T), T)
        vh = at(region(NT * GDV), NT, GDV)
        rh = at(region(2 * T), 2, T)
        Q1, K1, QK2, Q3, K4 = (at(region(T), T) for _ in range(5))
        o_dT, o_eT = region(T), region(T)
        dT, eT = at(o_dT, T), at(o_eT, T)
        gsq = at(o_dT, GDV)
        q3p = at(o_dT + 256, DB, NS)
        o8 = at(o_dT + 512, GDV)
        atS = at(o_dT + 768, NS)
        k4T = [at(o_dT + 800 + i * P, P) for i in range(2)]
        k4p = at(o_eT, DB, P)
        uT = at(o_SC, T)
        rst = at(o_SC + T, T)
        S0 = at(o_SC + 2 * T, DB, GDV)
        Sp = at(region(GDV), GDV)
        atb = [at(region(P), P) for _ in range(2)]
        sig = [Bc[:, i * W3:(i + 1) * W3] for i in range(2)]
        wgu = at(region(4 * P), 4 * P)
        print("gla top", top[0])
        assert top[0] <= ARENA
        o_zT = o_SC2 + 4484 + T + 4 * T + KD * T
        zT = at(o_zT, KD, T)
        msg = [arena[:, o_zT + KD * T + i * W3:][:, 0:W3] for i in range(6)]
        top[0] = base
        x2 = at(region(NT * D), NT, D)
        o_act = top[0]
        actT = at(region(KF * T), KF, T)
        fsig = [at(region(W3), W3) for _ in range(2)]
        ft = [at(region(W3), W3) for _ in range(2)]
        print("ffn top", top[0])
        assert top[0] <= ARENA
        assert o_zT >= base + NT * D
        xr = [arena[:, o_zT + KD * T + i * D:][:, 0:D] for i in range(4)]
        h2 = [arena[:, o_zT + KD * T + 4 * D + i * D:][:, 0:D] for i in range(2)]
        sqj2 = arena[:, o_zT + KD * T + 6 * D:][:, 0:D]
        assert o_zT + KD * T + 7 * D <= ARENA
        yT = hT
        gfb = arena[:, o_act:o_act + D]
        yo = [arena[:, o_act + (1 + i) * D:o_act + (2 + i) * D] for i in range(3)]

        scr = nc.dram_tensor("near_bias_rows", [DH, P * 384], F32, kind="Internal").ap()

        c_landed = sem("c_landed")
        x_landed = [sem(f"x_landed{i}") for i in range(4)]
        x_used = sem("x_used")
        x_sq, x_ms, x_rt, x_h = sem("x_sq"), sem("x_ms"), sem("x_rt"), sem("x_h")
        relx_done, nb_in = sem("relx_done"), sem("nb_in")
        nb_out = [sem(f"nb_out{i}") for i in range(2)]
        zeroed = sem("zeroed")
        kv_done, krt_done, kn_done = sem("kv_done"), sem("krt_done"), sem("kn_done")
        pg_landed = sem("pg_landed")
        qis_done = sem("qis_done")
        rl_full, rl_used = sem("rl_full"), sem("rl_used")
        sc_done, sc_diag = sem("sc_done"), sem("sc_diag")
        wr_done, rs_done, rsw_done = sem("wr_done"), sem("rs_done"), sem("rsw_done")
        mask_done = sem("mask_done")
        kt_out = [sem(f"kt_out{i}") for i in range(2)]
        ki_out = sem("ki_out")
        outs = sem("outs")
        near_done = sem("near_done")
        lg_full, lg_used = sem("lg_full"), sem("lg_used")
        mx_done, pr_done = sem("mx_done"), sem("pr_done")
        pt_done = sem("pt_done")
        ks_landed = [sem(f"ks_landed{i}") for i in range(2)]
        vs_landed = sem("vs_landed")
        qbs_done, relt_done = sem("qbs_done"), sem("relt_done")
        smx, spr, spn, som = sem("smx"), sem("spr"), sem("spn"), sem("som")
        so_used = sem("so_used")
        wgu_in, st_in, st_out = sem("wgu_in"), sem("st_in"), sem("st_out")
        u_done, sp_done, b_done = sem("u_done"), sem("sp_done"), sem("b_done")
        d_done, e_done, f_done = sem("d_done"), sem("e_done"), sem("f_done")
        sg_done = sem("sg_done")
        q3p_done, k4p_done = sem("q3p_done"), sem("k4p_done")
        oss_done, oms_done, ort_done, on_done = sem("oss_done"), sem("oms_done"), sem("ort_done"), sem("on_done")
        core_done = sem("core_done")
        m_sig, m_a, m_b = sem("m_sig"), sem("m_a"), sem("m_b")
        r_landed = [sem(f"r_landed{i}") for i in range(4)]
        r_used = sem("r_used")
        y_sq, y_ms, y_rt, y_h = sem("y_sq"), sem("y_ms"), sem("y_rt"), sem("y_h")
        f_sig, f_t = sem("f_sig"), sem("f_t")
        g_landed = sem("g_landed")
        z_sq, z_ms, z_rt, z_o = sem("z_sq"), sem("z_ms"), sem("z_rt"), sem("z_o")
        z_x = sem("z_x")
        z_out = [sem(f"z_out{i}") for i in range(3)]
        act_seq, dve_seq, pool_seq = sem("act_seq"), sem("dve_seq"), sem("pool_seq")

        N_CONST = 11

        def all_nb_out(eng):
            for s_ in nb_out:
                eng.wait_ge(s_, 16 * DH // 2)

        def all_kt_out(eng):
            eng.wait_ge(kt_out[0], 16 * ((NT + 1) // 2))
            eng.wait_ge(kt_out[1], 16 * (NT // 2))

        xp, xs = a["x_prompt"][0], a["x_sample"].rearrange("b t d -> (b t) d")

        def x_src(i):
            return xp[i * P:(i + 1) * P, :] if i < NTP else xs

        block = ctx.enter_context(nc.Block())

        def load_w(sp, n):
            name, parts, w, k = units[n]
            if n >= 2:
                wait_full(sp, *last_chunk[units[n - 2][0]])
            if parts is None:
                f = name[1]
                v = wview(name)
                for src, c0, k0, kn_ in (("w_in", COL["gg"] + P * f, 0, KD), ("w_gla_branch", P * f, 8, KD),
                                         ("w_in", COL["gd"] + P * f, 16, KD), ("w_dsa_branch", P * f, 24, 4)):
                    sp.dma_start(v[:, k0:k0 + kn_, :], wsrc(src, c0, P, kn_)).then_inc(w_landed[n % 2], 16)
            else:
                for src, c0, c, d0 in parts:
                    sp.dma_start(wview(name)[:, :, d0:d0 + c], wsrc(src, c0, c, k)).then_inc(w_landed[n % 2], 16)

        @block.sync
        def _(sp):
            sp.dma_start(arena[:, o_c128:o_c128 + n128], a["c128"]).then_inc(c_landed, 16)
            for i in range(NT):
                if i == 3:
                    sp.dma_start(arena[0:32, o_c32:o_c32 + n32], a["c32"]).then_inc(c_landed, 16)
                    sp.dma_start(bits, a["cbits"]).then_inc(c_landed, 16)
                    sp.dma_start(vrow[0:8, :], a["g_mix"].rearrange("l (k p) -> (l k) p", p=P)).then_inc(c_landed, 16)
                    sp.dma_start(vrow[8:16, :], a["g_ffn"].rearrange("l (k p) -> (l k) p", p=P)).then_inc(c_landed, 16)
                    sp.dma_start(vrow[16:20, :], a["b_gate"].rearrange("l (k p) -> (l k) p", p=P)).then_inc(c_landed, 16)
                    sp.dma_start(vrow[20:22, :], a["gla_norm_g"].rearrange("l (k p) -> (l k) p", p=P)).then_inc(c_landed, 16)
                    sp.dma_start(relb[0:NB, :], a["rel_bias"]).then_inc(c_landed, 16)
                    sp.dma_start(kg_b, a["idx_k_g"].to_broadcast([P, IDM])).then_inc(c_landed, 16)
                    sp.dma_start(kb_b, a["idx_k_b"].to_broadcast([P, IDM])).then_inc(c_landed, 16)
                    sp.dma_start(pagetab[0:1, :], a["page_table"].rearrange("(o b) g -> o (b g)", o=1)).then_inc(c_landed, 16)
                    load_w(sp, 0)
                if i >= 4:
                    sp.wait_ge(x_used, i - 3)
                sp.dma_start(xa[i % 4][0:rows(i), :], x_src(i)).then_inc(x_landed[i % 4], 16)
            n_wo = unit_no[("wo", 0)]
            for n in range(1, len(units)):
                load_w(sp, n)
                if n == n_wo + 1:
                    for i in range(NT):
                        if i == 0:
                            wait_evac(sp, "mz", KD - 1, 2)
                            sp.wait_ge(m_b, 3 * KD)
                            sp.wait_ge(st_out, 32 * GH)
                        if i >= 4:
                            sp.wait_ge(r_used, 2 * (i - 3))
                        sp.dma_start(xr[i % 4][0:rows(i), :], x_src(i)).then_inc(r_landed[i % 4], 16)

        @block.tensor
        def _(pe):
            def begin(*key):
                c = chunk[key]
                if c >= 4:
                    pe.wait_ge(evac[c % 4], c // 4)
                return ring[:, c % 4, :]

            def done(ins, *key):
                ins.then_inc(full[chunk[key] % 4], 1)

            def feature_major(key, w, c0, m, n, src=hT, k=KD):
                ps = begin(*key)
                t0, tn = TCH[n]
                for kk in range(k):
                    ins = pe.matmul(ps[0:m, 0:tn], w[:, kk, c0:c0 + m], src[:, kk, t0:t0 + tn],
                                    start=kk == 0, stop=kk == k - 1)
                done(ins, *key)

            def token_major(key, w, c0, m, i, src=hT, k=KD):
                ps = begin(*key)
                for kk in range(k):
                    ins = pe.matmul(ps[0:rows(i), 0:m], src[:, kk, i * P:i * P + rows(i)], w[:, kk, c0:c0 + m],
                                    start=kk == 0, stop=kk == k - 1)
                done(ins, *key)

            def transposes(key, pairs, m=P):
                ps = begin(*key)
                for c, src in pairs:
                    k = src.shape[0]
                    ins = pe.transpose(ps[0:src.shape[1], c:c + k], src, ident[0:k, 0:k])
                done(ins, *key)

            pe.wait_ge(c_landed, 16 * N_CONST)
            transposes(("vec",), [(0, vrow[0:22, :])])
            for i in range(NT):
                pe.wait_ge(x_h, i + 1)
                for c in range(2):
                    transposes(("h", i, c), [(P * s, xa[i % 4][0:rows(i), (4 * c + s) * P:(4 * c + s + 1) * P])
                                             for s in range(4)])
            pe.wait_ge(relx_done, 1)
            for h in range(DH):
                ps = begin("nb", h)
                done(pe.matmul(ps[:, 0:383], relx[0:NB, h, :], k32["onehot"][:, 4:OHW], start=True, stop=True),
                     "nb", h)

            for i in range(NT):
                wait_evac(pe, "h", i, 1)
            wait_evac(pe, "h", NT - 1, 0)
            wait_w(pe, "idx")
            w = wview("idx")
            for f in range(2):
                for n in range(3):
                    feature_major(("qi", f, n), w, f * P, P, n)
            for i in range(NT):
                token_major(("ki", i), w, 256, 68, i)
            for n in range(3):
                ps = begin("al", n)
                for kk in range(KD):
                    ins = pe.matmul(ps[0:RANK, 0:W3], w[:, kk, 324:340], hT[:, kk, n * W3:(n + 1) * W3],
                                    start=kk == 0, stop=kk == KD - 1)
                done(ins, "al", n)
            pe.wait_ge(kn_done, 1)
            for n in range(3):
                transposes(("kiT", n), [(P * s, kn[0:rows(4 * n + s), 4 * n + s, :])
                                        for s in range(4 if n < 2 else 1)])
            pe.wait_ge(pg_landed, 16 * 32)
            for n in range(4):
                transposes(("ps", n), [(P * s, kpg[:, 4 * n + s, :]) for s in range(4)])
            for n in range(3):
                wait_evac(pe, "kiT", n)
                wait_evac(pe, "qi", 0, n)
                wait_evac(pe, "qi", 1, n)
            for b, h, c0, w_ in SCC:
                ps = begin("sc", b, h, c0, w_)
                q0 = 64 * (h % 2)
                done(pe.matmul(ps[:, 0:w_], qiT[q0:q0 + 64, h // 2, b * P:(b + 1) * P],
                               kiT[q0:q0 + 64, c0:c0 + w_], start=True, stop=True), "sc", b, h, c0, w_)
            pe.wait_ge(qis_done, 1)
            for n in range(4):
                wait_evac(pe, "ps", n)
            for g in range(2):
                ps = begin("wr", g)
                done(pe.matmul(ps[:, 0:IH], k32["exp_i"][:, g * P:(g + 1) * P], kw[0:NS, NTP, 64:68],
                               start=True, stop=True), "wr", g)
                ps = begin("si", g)
                for j in range(4):
                    b = 4 * g + j
                    for c0, cn, rhs in ((0, PAST, lambda: kiS[:, b, :]),
                                        (PAST, DT, lambda: kiT[:, SEQ + b * DT:SEQ + (b + 1) * DT])):
                        for hp in range(2):
                            ins = pe.matmul(ps[32 * j:32 * j + 32, c0:c0 + cn], qiS[:, 2 * b + hp, :], rhs(),
                                            start=hp == 0, stop=hp == 1)
                done(ins, "si", g)
            ps = begin("ss")
            for g in range(2):
                pe.wait_ge(rsw_done, g + 1)
                ins = pe.matmul(ps[0:NS, 0:NKS], k128["sum_i"][:, g * NS:(g + 1) * NS],
                                (rs_s, rl[0][:, 0:NKS])[g], start=g == 0, stop=g == 1)
            done(ins, "ss")

            for name in ("qd", "kd"):
                wait_w(pe, name)
                for f in range(4):
                    for n in range(3):
                        feature_major((name, f, n), wview(name), f * P, P, n)
            for f in range(4):
                for n in range(3):
                    wait_evac(pe, "kd", f, n)
            for i in range(NT):
                ps = begin("kt", i)
                for f in range(4):
                    ins = pe.transpose(ps[0:rows(i), f * P:(f + 1) * P], kdT[:, f, i * P:i * P + rows(i)], ident)
                done(ins, "kt", i)
            wait_w(pe, "vd")
            for i in range(NT):
                token_major(("vd", i), wview("vd"), 0, 512, i)

            def qk(u):
                b, h = UN[u]
                if u >= 2:
                    pe.wait_ge(lg_used, u - 1)
                p0 = 64 * (h % 2)
                L = P * (b + 1)
                for c0 in range(0, L, 512):
                    c1 = min(L, c0 + 512)
                    ins = pe.matmul(lgt[u % 2][:, c0:c1], qdT[p0:p0 + 64, h // 2, b * P:(b + 1) * P],
                                    kdT[p0:p0 + 64, h // 2, c0:c1], start=True, stop=True)
                ins.then_inc(lg_full, 1)

            def pv(u):
                b, h = UN[u]
                for c in range((b + 4) // 4):
                    wait_evac(pe, "pt", u, c)
                ps = begin("o", u)
                for s in range(b + 1):
                    ins = pe.matmul(ps[:, 0:DHD], pT[u % 2][:, s, :], vd[:, s, h * DHD:(h + 1) * DHD],
                                    start=s == 0, stop=s == b)
                done(ins, "o", u)
                if h == DH - 1:
                    wait_evac(pe, "o", u)
                    wait_evac(pe, "o", u - 1)
                    wait_evac(pe, "o", u - 2)
                    wait_evac(pe, "o", u - 3)
                    transposes(("ot", b), [(P * f, osb[b % 2][:, f * P:(f + 1) * P]) for f in range(4)])

            for n in range(3):
                for f in range(4):
                    wait_evac(pe, "qd", f, n)
            for i in range(NT):
                wait_evac(pe, "vd", i)
            qk(0)
            for u in range(len(UN) + 1):
                if u + 1 < len(UN):
                    qk(u + 1)
                if u >= 1:
                    pv(u - 1)
                if u < len(UN):
                    b = UN[u][0]
                    pe.wait_ge(pr_done, u + 1)
                    for c in range((b + 4) // 4):
                        transposes(("pt", u, c), [(P * (s - 4 * c), pr[u % 2][:, s * P:(s + 1) * P])
                                                  for s in range(4 * c, min(b + 1, 4 * c + 4))])

            pe.wait_ge(qbs_done, 1)
            pe.wait_ge(relt_done, 1)
            for g in range(2):
                for j in range(4):
                    b = 4 * g + j
                    pe.wait_ge(ks_landed[b % 2], 32 * (b // 2 + 1))
                    for p in range(NPG):
                        ps = begin("kp", g, j, p)
                        for f in range(4):
                            ins = pe.transpose(ps[:, f * P:(f + 1) * P], kpS[b % 2][:, p, f * P:(f + 1) * P], ident)
                        done(ins, "kp", g, j, p)
                    for p in range(NPG):
                        wait_evac(pe, "kp", g, j, p)
                    if j == 0:
                        pe.wait_ge(lg_used, len(UN))
                    for c0, cn in ((0, PAST), (PAST, DT)):
                        for f in range(4):
                            rhs = kTs[b % 2][:, f, :] if cn == PAST else kdT[:, f, SEQ + b * DT:SEQ + (b + 1) * DT]
                            ins = pe.matmul(lgt[g][32 * j:32 * j + 32, c0:c0 + cn], qbS[:, 4 * b + f, :], rhs,
                                            start=f == 0, stop=f == 3)
                    ins.then_inc(so_used, 1)
                ps = begin("mb", g)
                pe.matmul(ps[:, 0:NKS], k32["exp_h"][:, g * P:(g + 1) * P], scs[0:NS, :], start=True, stop=False)
                for t in range(DT):
                    ins = pe.matmul(ps[:, 0:NKS], relt[0:NB, t, :], k32["onehot"][:, 3 - t:3 - t + NKS],
                                    start=False, stop=t == DT - 1)
                done(ins, "mb", g)
            for g in range(2):
                pe.wait_ge(spn, g + 1)
                ps = begin("sl", g)
                done(pe.transpose(ps[0:NS, 0:P], pnS.rearrange("p a b -> p (a b)"), ident), "sl", g)
                transposes(("spt", g), [(P * p, prS[g][:, p * P:(p + 1) * P]) for p in range(NPG)])
                wait_evac(pe, "sl", g)
                wait_evac(pe, "spt", g)
                pe.wait_ge(vs_landed, 16 * 8 * (g + 1))
                ps = begin("so", g)
                for j in range(4):
                    for p in range(NPG):
                        pe.matmul(ps[32 * j:32 * j + 32, :], ptS[:, p, 32 * j:32 * j + 32], vpS[j][:, p, :],
                                  start=p == 0, stop=False)
                    ins = pe.matmul(ps[32 * j:32 * j + 32, :], ptS[0:NS, 2, 32 * j:32 * j + 32], vd[0:NS, NTP, :],
                                    start=False, stop=True)
                done(ins, "so", g)
                wait_evac(pe, "so", g)
                ps = begin("sot", g)
                for f in range(4):
                    ins = pe.matmul(ps[:, 16 * f:16 * f + 16], omS[:, f * P:(f + 1) * P], k128["sum_t"],
                                    start=True, stop=True)
                done(ins, "sot", g)

            def turn_outputs(h):
                for i in range(NT):
                    pe.wait_ge(on_done, NT * h + i + 1)
                    transposes(("gt", h, i), [(P * f, (vh[:, i, :] if i < NTP else o8[0:NS, :])[:, f * P:(f + 1) * P])
                                              for f in range(2)])

            def pair_products(h, i):
                t0 = i * P
                ps = begin("at", h, i)
                if i == NTP:
                    ins = pe.matmul(ps[0:NS, 0:NS], K1[:, t0:T], Q3[:, t0:T], start=True, stop=True)
                else:
                    pe.matmul(ps[0:64, 0:64], K1[:, t0:t0 + 64], Q1[:, t0:t0 + 64], start=True, stop=True)
                    pe.matmul(ps[0:64, 64:P], QK2[:, t0:t0 + 64], QK2[:, t0 + 64:t0 + P], start=True, stop=True)
                    ins = pe.matmul(ps[64:P, 64:P], K1[:, t0 + 64:t0 + P], Q1[:, t0 + 64:t0 + P],
                                    start=True, stop=True)
                done(ins, "at", h, i)
                ps = begin("k4", h, i)
                done(pe.transpose(ps[0:rows(i), 0:P], K4[:, t0:t0 + rows(i)], ident), "k4", h, i)

            for h in range(GH):
                wait_w(pe, ("qkv", h))
                w = wview(("qkv", h))
                for f, key in enumerate(("gq", "gk")):
                    for n in range(3):
                        feature_major((key, h, n), w, f * GDK, GDK, n)
                if h >= 1:
                    turn_outputs(h - 1)
                pe.wait_ge(wgu_in, 16)
                for n in range(3):
                    ps = begin("gz", h, n)
                    done(pe.matmul(ps[:, 0:W3], wgu[0:RANK, h * GDK:(h + 1) * GDK],
                                   alT[0:RANK, n * W3:(n + 1) * W3], start=True, stop=True), "gz", h, n)
                for i in range(NT):
                    token_major(("gv", h, i), w, 2 * GDK, GDV, i)
                wait_w(pe, ("r", h))
                w = wview(("r", h))
                for f in range(2):
                    for n in range(3):
                        feature_major(("gr", h, f, n), w, f * P, P, n)
                pe.wait_ge(f_done, 5 * (h + 1))
                for i in range(NT):
                    wait_evac(pe, "gv", h, i)
                pair_products(h, 0)
                for i in range(NTP):
                    pair_products(h, i + 1)
                    ps = begin("go", h, i)
                    wait_evac(pe, "at", h, i)
                    ins = pe.matmul(ps[:, 0:GDV], atb[i % 2], vh[:, i, :], start=True, stop=i == 0)
                    if i >= 1:
                        wait_evac(pe, "ds", h, i - 1)
                        ins = pe.matmul(ps[:, 0:GDV], Q3[:, i * P:(i + 1) * P], Sp, start=False, stop=True)
                    done(ins, "go", h, i)
                    wait_evac(pe, "k4", h, i)
                    ps = begin("ds", h, i)
                    done(pe.matmul(ps[:, 0:GDV], k4T[i % 2], vh[:, i, :], start=True, stop=True), "ds", h, i)
                ps = begin("go", h, NTP)
                wait_evac(pe, "at", h, NTP)
                pe.wait_ge(q3p_done, h + 1)
                pe.wait_ge(st_in, 16 * (h + 1))
                pe.matmul(ps[0:NS, 0:GDV], atS[0:NS, :], vh[0:NS, NTP, :], start=True, stop=False)
                for b in range(DB):
                    ins = pe.matmul(ps[0:NS, 0:GDV], q3p[:, b, :], S0[:, b, :], start=False, stop=b == DB - 1)
                done(ins, "go", h, NTP)
                pe.wait_ge(k4p_done, h + 1)
                for b in range(DB):
                    ps = begin("ds", h, NTP + b)
                    done(pe.matmul(ps[:, 0:GDV], k4p[0:NS, b, :], vh[0:NS, NTP, :], start=True, stop=True),
                         "ds", h, NTP + b)
            turn_outputs(GH - 1)

            for i in range(NT):
                wait_evac(pe, "gt", GH - 1, i)
            for f in range(KD):
                wait_w(pe, ("m", f))
                w = wview(("m", f))
                for n in range(3):
                    feature_major(("mg", f, n), w, 0, P, n)
                    feature_major(("my", f, n), w[:, 8:16, :], 0, P, n, src=ogT)
                    feature_major(("me", f, n), w[:, 16:24, :], 0, P, n)
                    feature_major(("mz", f, n), w[:, 24:28, :], 0, P, n, src=odT, k=4)
            pe.wait_ge(m_b, 3 * KD)
            wait_w(pe, ("wo", 0))
            wait_w(pe, ("wo", 1))

            def h2_tile(i):
                pe.wait_ge(y_h, i + 1)
                for c in range(2):
                    transposes(("h2", i, c), [(P * s, h2[i % 2][0:rows(i), (4 * c + s) * P:(4 * c + s + 1) * P])
                                              for s in range(4)])
            for i in range(NT):
                for s in range(2):
                    token_major(("wo", i, s), wview(("wo", s)), 0, 512, i, src=zT)
                if i >= 2:
                    h2_tile(i - 2)
            h2_tile(NT - 2)
            h2_tile(NT - 1)
            for i in range(NT):
                wait_evac(pe, "h2", i, 1)
            wait_evac(pe, "h2", NT - 1, 0)
            for f in range(KF):
                if f % 2 == 0:
                    wait_w(pe, ("ff", f // 2))
                w = wview(("ff", f // 2))
                for n in range(3):
                    feature_major(("fg", f, n), w, P * (f % 2), P, n)
                    feature_major(("fu", f, n), w, 256 + P * (f % 2), P, n)
            for n in range(3):
                wait_evac(pe, "fu", KF - 1, n)
            for f in range(KD):
                wait_w(pe, ("dn", f))
                for n in range(3):
                    feature_major(("dn", f, n), wview(("dn", f)), 0, P, n, src=actT, k=KF)
            for f in range(KD):
                for n in range(3):
                    wait_evac(pe, "dn", f, n)
            for i in range(NT):
                for c in range(2):
                    ps = begin("yt", i, c)
                    for s in range(4):
                        ins = pe.transpose(ps[0:rows(i), s * P:(s + 1) * P],
                                           yT[:, 4 * c + s, i * P:i * P + rows(i)], ident)
                    done(ins, "yt", i, c)

        @block.scalar
        def _(act):
            seq = [0]

            def link(ins):
                seq[0] += 1
                ins.then_inc(act_seq, 1)
                act.wait_ge(act_seq, seq[0])

            def copy_out(dst, src, *key, scale=1.0):
                wait_full(act, *key)
                evacuates(act.activation(dst, src, ACT.Copy, scale=scale), *key)

            act.wait_ge(c_landed, 16 * N_CONST)
            copy_out(vec, bank("vec")[:, 0:22], "vec")
            for i in range(NT + 1):
                if i < NT:
                    r = rows(i)
                    act.wait_ge(x_landed[i % 4], 16 * (i // 4 + 1))
                    if i >= 1:
                        act.wait_ge(x_sq, i)
                    act.activation(sqj[0:r, :], xa[i % 4][0:r, :], ACT.Square,
                                   accum_out=ssq[0:r, i:i + 1]).then_inc(x_sq, 1)
                if i >= 1:
                    r = rows(i - 1)
                    act.wait_ge(x_ms, i)
                    act.activation(rt[0:r, i - 1:i], msq[0:r, i - 1:i], ACT.Sqrt).then_inc(x_rt, 1)
            for f in range(2):
                for n in range(3):
                    copy_out(qiT[:, f, n * W3:(n + 1) * W3], bank("qi", f, n)[:, 0:W3], "qi", f, n)
            act.wait_ge(zeroed, 1)
            for i in range(NT):
                copy_out(kw[0:rows(i), i, :], bank("ki", i)[0:rows(i), 0:68], "ki", i)
            for n in range(3):
                copy_out(alT[0:RANK, n * W3:(n + 1) * W3], bank("al", n)[0:RANK, 0:W3], "al", n)
            act.wait_ge(kv_done, 1)
            act.activation(krt, kvar, ACT.Sqrt).then_inc(krt_done, 1)
            for n in range(3):
                w_ = 512 if n < 2 else NS
                copy_out(kiT[:, n * 512:n * 512 + w_], bank("kiT", n)[:, 0:w_], "kiT", n)
            for n in range(4):
                copy_out(kiS[:, 2 * n:2 * n + 2, :], bank("ps", n).rearrange("p (a b) -> p a b", a=2), "ps", n)
            for n, key in enumerate(SCC):
                if n >= 2:
                    act.wait_ge(rl_used, n - 1)
                wait_full(act, "sc", *key)
                w_ = key[3]
                evacuates(act.activation(rl[n % 2][:, 0:w_], bank("sc", *key)[:, 0:w_], ACT.Relu, scale=0.0625),
                          "sc", *key)
            for g in range(2):
                wait_full(act, "si", g)
                if g == 1:
                    act.wait_ge(rl_used, len(SCC))
                evacuates(act.activation((rs_s, rl[0][:, 0:NKS])[g], bank("si", g)[:, 0:NKS], ACT.Relu,
                                         scale=0.0625), "si", g)
            act.wait_ge(x_h, NT)
            for name, dst, sc in (("qd", qdT, 0.125), ("kd", kdT, 1.0)):
                for f in range(4):
                    for n in range(3):
                        if name == "qd" and f == 0 and n == 0:
                            wait_evac(act, "h", NT - 1, 0)
                            wait_evac(act, "h", NT - 1, 1)
                        copy_out(dst[:, f, n * W3:(n + 1) * W3], bank(name, f, n)[:, 0:W3], name, f, n, scale=sc)
            for i in range(NT):
                if i >= 2:
                    act.wait_ge(kt_out[i % 2], 16 * (i // 2))
                copy_out(kst[i % 2][0:rows(i), :], bank("kt", i)[0:rows(i), :], "kt", i)
            all_nb_out(act)
            for i in range(NT):
                copy_out(vd[0:rows(i), i, :], bank("vd", i)[0:rows(i), :], "vd", i)
            all_kt_out(act)
            for u, (b, h) in enumerate(UN):
                L = P * (b + 1)
                act.wait_ge(mx_done, u + 1)
                if u >= 2:
                    for c in range((UN[u - 2][0] + 4) // 4):
                        wait_evac(act, "pt", u - 2, c)
                link(act.activation(pr[u % 2][:, 0:L], nlg[u % 2][:, 0:L], ACT.Exp, bias=nmx[:, u % 4:u % 4 + 1],
                                    scale=-1.0, accum_out=rsum[:, u % 4:u % 4 + 1]))
                act.sem_inc(pr_done, 1)
                if b >= 4:
                    if u >= 2:
                        wait_full(act, "o", u - 2)
                    k = b - 3
                    copy_out(pT[u % 2][:, 4:4 + k, :], bank("pt", u, 1)[:, 0:k * P].rearrange("p (a b) -> p a b", b=P),
                             "pt", u, 1)
                if h == 0 and b >= 1:
                    copy_out(odT[:, :, (b - 1) * P:b * P], bank("ot", b - 1).rearrange("p (a b) -> p a b", a=4),
                             "ot", b - 1)
            copy_out(odT[:, :, SEQ - P:SEQ], bank("ot", NTP - 1).rearrange("p (a b) -> p a b", a=4), "ot", NTP - 1)
            def sample_exp(g):
                act.wait_ge(smx, g + 1)
                act.activation(prS[g], nlS[g], ACT.Exp, bias=nmx[:, g:g + 1], scale=-1.0,
                               accum_out=rsum[:, g:g + 1]).then_inc(spr, 1)

            for g in range(2):
                for j in range(4):
                    b = 4 * g + j
                    if b >= 2:
                        act.wait_ge(so_used, b - 1)
                    for p in range(NPG):
                        copy_out(kTs[b % 2][:, :, p * P:(p + 1) * P],
                                 bank("kp", g, j, p).rearrange("p (a b) -> p a b", a=4), "kp", g, j, p)
                copy_out(mbS[g], bank("mb", g)[:, 0:NKS], "mb", g)
                if g == 1:
                    sample_exp(0)
            sample_exp(1)
            for g in range(2):
                if g == 1:
                    wait_full(act, "so", 0)
                copy_out(ptS[0:NS, 2, :], bank("sl", g)[0:NS, 0:P], "sl", g)
                copy_out(ptS[:, 0:2, :], bank("spt", g)[:, 0:2 * P].rearrange("p (a b) -> p a b", b=P), "spt", g)
                copy_out(odT[:, :, SEQ + 16 * g:SEQ + 16 * g + 16],
                         bank("sot", g)[:, 0:64].rearrange("p (a b) -> p a b", a=4), "sot", g)
            nsg = 0
            for h in range(GH):
                if h >= 1:
                    act.wait_ge(f_done, 5 * h)
                for key, dst in (("gq", qh), ("gk", kh)):
                    for n in range(3):
                        copy_out(dst[:, n * W3:(n + 1) * W3], bank(key, h, n)[:, 0:W3], key, h, n)
                for n in range(3):
                    wait_full(act, "gz", h, n)
                    ins = act.activation(uT[:, n * W3:(n + 1) * W3], bank("gz", h, n)[:, 0:W3], ACT.Identity,
                                         bias=vec[:, 16 + h:17 + h])
                    evacuates(ins, "gz", h, n)
                for n in range(3):
                    wait_evac(act, "gz", h, n)
                link(act.activation(eT, uT, ACT.Abs))
                link(act.activation(eT, eT, ACT.Exp, scale=-1.0))
                act.activation(eT, eT, ACT.Ln, bias=one).then_inc(sp_done, 1)
                if h >= 1:
                    wait_full(act, "gt", h - 1, NTP)
                for m in range(NT):
                    r = rows(m)
                    copy_out(vh[0:r, m, :], bank("gv", h, m)[0:r, 0:GDV], "gv", h, m)
                    if m >= 5:
                        continue
                    act.wait_ge(d_done, 5 * h + m + 1)
                    if m >= 1:
                        act.wait_ge(f_done, 5 * h + m)
                    if m == 2:
                        act.activation(eT[:, 0:SEQ].rearrange("p (c s) -> p c s", s=P)[:, :, 0:64],
                                       dT[:, 0:SEQ].rearrange("p (c s) -> p c s", s=P)[:, :, 0:64],
                                       ACT.Exp, scale=-1 / 16)
                        act.activation(eT[:, 0:SEQ].rearrange("p (c s) -> p c s", s=P)[:, :, 64:P],
                                       dT[:, 0:SEQ].rearrange("p (c s) -> p c s", s=P)[:, :, 64:P],
                                       ACT.Exp, scale=1 / 16).then_inc(e_done, 1)
                    else:
                        act.activation(eT, Bc if m == 3 else dT, ACT.Exp,
                                       scale=(1 / 16, -1 / 16, 0, 1 / 16, -1 / 16)[m]).then_inc(e_done, 1)
                for f in range(2):
                    for n in range(3):
                        wait_full(act, "gr", h, f, n)
                        if nsg >= 2:
                            k = nsg - 2
                            wait_evac(act, "gr", k // 6, k % 6 // 3, k % 3)
                        act.activation(sig[nsg % 2], bank("gr", h, f, n)[:, 0:W3], ACT.Sigmoid).then_inc(sg_done, 1)
                        nsg += 1

                def turned_keys(i):
                    if 2 <= i < NTP:
                        wait_full(act, "ds", h, i - 2)
                    if i == NTP:
                        wait_full(act, "ds", h, NTP - 2)
                    copy_out(k4T[i % 2][0:rows(i), :], bank("k4", h, i)[0:rows(i), 0:P], "k4", h, i)

                turned_keys(0)
                for i in range(NTP):
                    turned_keys(i + 1)
                    wait_full(act, "ds", h, i)
                    copy_out(vh[:, i, :], bank("go", h, i)[:, 0:GDV], "go", h, i)
                copy_out(o8[0:NS, :], bank("go", h, NTP)[0:NS, 0:GDV], "go", h, NTP)
                for i in range(NT):
                    wait_evac(act, "go", h, i)
                    r = rows(i)
                    src = vh[:, i, :] if i < NTP else o8[0:r, :]
                    if i >= 1:
                        act.wait_ge(act_seq, seq[0])
                    seq[0] += 1
                    act.activation(gsq[0:r, :], src, ACT.Square, accum_out=oss[0:r, i:i + 1]).then_inc(act_seq, 1)
                act.wait_ge(act_seq, seq[0])
                act.sem_inc(oss_done, 1)
                act.wait_ge(oms_done, h + 1)
                act.activation(ort, oms, ACT.Sqrt).then_inc(ort_done, 1)
            m = 0
            for f in range(KD):
                for n in range(3):
                    if m >= 2:
                        act.wait_ge(m_b, m - 1)
                    for w, k in (("mg", 0), ("me", 1)):
                        wait_full(act, w, f, n)
                        evacuates(act.activation(msg[2 * (m % 2) + k], bank(w, f, n)[:, 0:W3], ACT.Sigmoid), w, f, n)
                    m += 1
            act.wait_ge(st_out, 32 * GH)
            for i in range(NT):
                r = rows(i)
                act.wait_ge(r_used, 2 * (i + 1))
                link(act.activation(sqj2[0:r, :], x2[0:r, i, :], ACT.Square, accum_out=ssq[0:r, i:i + 1]))
                act.sem_inc(y_sq, 1)
                act.wait_ge(y_ms, i + 1)
                act.activation(rt[0:r, i:i + 1], msq[0:r, i:i + 1], ACT.Sqrt).then_inc(y_rt, 1)
            for m in range(3 * KF):
                f, n = m // 3, m % 3
                if m >= 2:
                    act.wait_ge(f_t, m - 1)
                wait_full(act, "fg", f, n)
                act.activation(fsig[m % 2], bank("fg", f, n)[:, 0:W3], ACT.Sigmoid).then_inc(f_sig, 1)
            for f in range(KD):
                for n in range(3):
                    copy_out(yT[:, f, n * W3:(n + 1) * W3], bank("dn", f, n)[:, 0:W3], "dn", f, n)
            for i in range(NT):
                r = rows(i)
                act.wait_ge(z_x, i + 1)
                if i >= 3:
                    act.wait_ge(z_out[i % 3], 16 * (i // 3))
                link(act.activation(yo[i % 3][0:r, :], x2[0:r, i, :], ACT.Square, accum_out=ssq[0:r, i:i + 1]))
                act.sem_inc(z_sq, 1)
                act.wait_ge(z_ms, i + 1)
                act.activation(rt[0:r, i:i + 1], msq[0:r, i:i + 1], ACT.Sqrt).then_inc(z_rt, 1)

        @block.vector
        def _(v):
            seq = [0]

            def link(ins):
                seq[0] += 1
                ins.then_inc(dve_seq, 1)
                v.wait_ge(dve_seq, seq[0])

            def bc(col, shape, axis):
                return col.unsqueeze(axis).to_broadcast(shape)

            link(v.memset(one, 1.0))
            link(v.memset(cnt, 1.0))
            v.wait_ge(c_landed, 16 * N_CONST)
            for h in range(DH):
                v.tensor_copy(relx[0:NB, h, :], relb[0:NB, h:h + 1].to_broadcast([NB, P]))
            link(v.memset(oss, 1.0))
            v.sem_inc(relx_done, 1)
            wait_evac(v, "vec")

            def mean_tile(i, s_sq, s_ms):
                r = rows(i)
                v.wait_ge(s_sq, i + 1)
                v.tensor_scalar(msq[0:r, i:i + 1], ssq[0:r, i:i + 1], 1.0 / D, EPS, ALU.mult, ALU.add).then_inc(s_ms, 1)

            def norm_tile(i, src, dst, s_rt, s_h):
                r = rows(i)
                v.wait_ge(s_rt, i + 1)
                link(v.reciprocal(rstd[0:r, i:i + 1], rt[0:r, i:i + 1]))
                v.tensor_scalar(dst[0:r, :], src[0:r, :], rstd[0:r, i:i + 1], None, ALU.mult).then_inc(s_h, 1)

            def turn_tile(i, gains, key, out):
                r = rows(i)
                for c in range(2):
                    wait_full(v, key, i, c)
                    g = gains[:, 4 * c:4 * c + 4].unsqueeze(2).to_broadcast([P, 4, r])
                    src = bank(key, i, c).rearrange("p (a b) -> p a b", a=4)[:, :, 0:r]
                    evacuates(v.tensor_tensor(out[:, 4 * c:4 * c + 4, i * P:i * P + r], src, g, ALU.mult), key, i, c)

            for i in range(NT + 2):
                if i < NT:
                    mean_tile(i, x_sq, x_ms)
                if 1 <= i <= NT:
                    norm_tile(i - 1, xa[(i - 1) % 4], xa[(i - 1) % 4], x_rt, x_h)
                if i >= 2:
                    turn_tile(i - 2, vec[:, 0:8], "h", hT)
                    v.sem_inc(x_used, 1)
            for h in range(DH):
                wait_full(v, "nb", h)
                link(v.tensor_copy(r31[:, h:h + 1], bank("nb", h)[:, 0:1]))
                if h >= 2:
                    v.wait_ge(nb_out[h % 2], 16 * (h // 2))
                evacuates(v.tensor_scalar(nbs[h % 2], bank("nb", h)[:, 0:383], r31[:, h:h + 1], None, ALU.subtract),
                          "nb", h)
            for i in range(NT):
                wait_evac(v, "ki", i)
            kv = kw[:, :, 0:IDM]
            link(v.tensor_reduce(kmu, kv, X, ALU.add))
            link(v.tensor_scalar(kmu, kmu, 1.0 / IDM, None, ALU.mult))
            link(v.tensor_tensor(kd2, kv, bc(kmu, [P, NT, IDM], 2), ALU.subtract))
            link(v.tensor_tensor(kn[:, :, 0:IDM], kd2, kd2, ALU.mult))
            link(v.tensor_reduce(kvar, kn[:, :, 0:IDM], X, ALU.add))
            link(v.tensor_scalar(kvar, kvar, 1.0 / IDM, EPS, ALU.mult, ALU.add))
            v.sem_inc(kv_done, 1)
            v.wait_ge(krt_done, 1)
            link(v.reciprocal(krs, krt))
            link(v.tensor_tensor(kd2, kd2, bc(krs, [P, NT, IDM], 2), ALU.mult))
            link(v.tensor_tensor(kd2, kd2, bc(kg_b, [P, NT, IDM], 1), ALU.mult))
            link(v.tensor_tensor(kn[:, :, 0:IDM], kd2, bc(kb_b, [P, NT, IDM], 1), ALU.add))
            link(v.tensor_tensor(kn[:, :, IDM:P], kd2, bc(kb_b, [P, NT, IDM], 1), ALU.add))
            v.sem_inc(kn_done, 1)
            v.wait_ge(zeroed, 2)
            for n in range(3):
                wait_evac(v, "qi", 0, n)
                wait_evac(v, "qi", 1, n)
            q4 = qiS.rearrange("p (b f) (h t) -> p b f h t", f=2, t=DT)
            for f in range(2):
                for e in range(2):
                    src = qiT[64 * e:64 * e + 64, f, SEQ:T].rearrange("p (b t) -> p b t", t=DT)
                    ins = v.tensor_copy(q4[64 * e:64 * e + 64, :, f, 2 * f + e, :], src)
            link(ins)
            v.sem_inc(qis_done, 1)
            for n, (b, h, c0, w_) in enumerate(SCC):
                wait_evac(v, "sc", b, h, c0, w_)
                dst = SC[:, SCAT[b] + c0:SCAT[b] + c0 + w_]
                wt = kw[:, b, 64 + h:65 + h]
                if h == 0:
                    ins = v.tensor_scalar(dst, rl[n % 2][:, 0:w_], wt, None, ALU.mult)
                else:
                    ins = v.scalar_tensor_tensor(dst, rl[n % 2][:, 0:w_], wt, dst, ALU.mult, ALU.add)
                ins.then_inc(rl_used, 1)
                v.wait_ge(rl_used, n + 1)
                if h == IH - 1 and c0 + w_ == P * (b + 1):
                    v.sem_inc(sc_done, 1)
            for g in range(2):
                wait_full(v, "wr", g)
                link(v.tensor_tensor(wtmp, bank("wr", g)[:, 0:IH], k128["pick_i"], ALU.mult))
                evacuates(v.tensor_reduce(wrow[:, g:g + 1], wtmp, X, ALU.add), "wr", g)
                wait_evac(v, "wr", g)
                wait_evac(v, "si", g)
                buf = (rs_s, rl[0][:, 0:NKS])[g]
                v.tensor_scalar(buf, buf, wrow[:, g:g + 1], None, ALU.mult).then_inc(rsw_done, 1)
            v.wait_ge(zeroed, 3)
            wait_full(v, "ss")
            link(v.tensor_copy(scs[0:NS, 0:PAST], bank("ss")[0:NS, 0:PAST]))
            evacuates(v.tensor_tensor(scs[0:NS, PAST:NKS], bank("ss")[0:NS, PAST:NKS], k32["future"], ALU.add), "ss")
            wait_evac(v, "ss")

            v.wait_ge(sc_diag, NTP - 2)
            spans = [(SCAT[b], P * (b + 1), 0.0) for b in range(2, NTP)] + [(_n, NKS, float(TOPK - TOPK_S))]
            GRP = [(0, 4), (4, 7)]
            link(v.memset(cand, 0))

            def count(k):
                s0, n_, init = spans[k]
                return v.tensor_scalar(junk[:, s0:s0 + n_], SC[:, s0:s0 + n_], cand[:, k:k + 1].bitcast(F32), init,
                                       ALU.is_ge, ALU.add, accum_out=cnt[:, k:k + 1])

            def try_bit(g, b):
                lo, hi = GRP[g]
                return v.tensor_scalar(cand[:, lo:hi], thr[:, lo:hi], bits[:, b], None, ALU.bitwise_xor)

            def keep(g, b):
                lo, hi = GRP[g]
                return v.tensor_scalar(gbit[:, lo:hi], cnt[:, lo:hi], float(TOPK), k128["bits_f"][:, b],
                                       ALU.is_ge, ALU.mult)

            def set_bit(g):
                lo, hi = GRP[g]
                return v.tensor_tensor(thr[:, lo:hi], thr[:, lo:hi], gbit[:, lo:hi], ALU.bitwise_xor)

            for k in range(7):
                ins = count(k)
            link(ins)
            link(v.tensor_scalar(thr, cnt, float(TOPK), 1.0, ALU.is_ge, ALU.subtract))
            link(try_bit(0, slice(0, 1)))
            link(try_bit(1, slice(0, 1)))
            for k in range(4):
                ins = count(k)
            link(ins)
            step0 = seq[0]
            PER = 10
            ROUNDS = 30

            with v.Fori(0, ROUNDS) as r:
                at_step = lambda n: v.wait_ge(dve_seq, r * PER + (step0 + n))
                inc_ = lambda ins: ins.then_inc(dve_seq, 1)
                inc_(count(4))
                at_step(0)
                inc_(keep(0, bass.ds(r, 1)))
                inc_(count(5))
                at_step(2)
                inc_(set_bit(0))
                inc_(count(6))
                at_step(4)
                inc_(try_bit(0, bass.ds(r + 1, 1)))
                at_step(6)
                count(0)
                count(1)
                inc_(keep(1, bass.ds(r, 1)))
                count(2)
                at_step(7)
                inc_(set_bit(1))
                at_step(8)
                inc_(try_bit(1, bass.ds(r + 1, 1)))
                inc_(count(3))
                at_step(9)
            seq[0] = step0 + ROUNDS * PER
            v.wait_ge(dve_seq, seq[0])
            for k in range(4, 7):
                ins = count(k)
            link(ins)
            for g in range(2):
                link(keep(g, slice(ROUNDS, ROUNDS + 1)))
                link(set_bit(g))

            def mask_step(k, n):
                s0, n_, init = spans[k]
                s_, t_ = SC[:, s0:s0 + n_], thr[:, k:k + 1].bitcast(F32)
                if n == 0:
                    link(v.tensor_scalar(inc[:, 0:n_], s_, t_, init, ALU.is_gt, ALU.add, accum_out=cnt[:, k:k + 1]))
                elif n == 1:
                    link(v.tensor_scalar(need[:, k:k + 1], cnt[:, k:k + 1], -1.0, float(TOPK), ALU.mult, ALU.add))
                    link(v.tensor_scalar(eqc[:, 0:n_], s_, t_, None, ALU.is_equal))
                elif n == 2:
                    link(v.tensor_tensor_scan(inc[:, 0:n_], eqc[:, 0:n_], eqc[:, 0:n_], 0.0, ALU.add, ALU.max))
                elif n == 3:
                    link(v.scalar_tensor_tensor(eqc[:, 0:n_], inc[:, 0:n_], need[:, k:k + 1], eqc[:, 0:n_],
                                                ALU.is_le, ALU.mult))
                elif n == 4:
                    link(v.scalar_tensor_tensor(inc[:, 0:n_], s_, t_, eqc[:, 0:n_], ALU.is_gt, ALU.max))
                elif n == 5:
                    link(v.tensor_scalar(s_, inc[:, 0:n_], 1.0, -NEG, ALU.subtract, ALU.mult))
                    v.sem_inc(mask_done, 1)

            v.wait_ge(nb_in, 16 * DH)
            wait_evac(v, "vd", NTP)
            all_kt_out(v)
            v.wait_ge(ki_out, 32)

            def norm_head(u):
                b, h = UN[u]
                wait_full(v, "o", u)
                link(v.reciprocal(rrec[:, u % 4:u % 4 + 1], rsum[:, u % 4:u % 4 + 1]))
                if h == 0 and b >= 2:
                    wait_full(v, "ot", b - 2)
                evacuates(v.tensor_scalar(osb[b % 2][:, h * DHD:(h + 1) * DHD], bank("o", u)[:, 0:DHD],
                                          rrec[:, u % 4:u % 4 + 1], None, ALU.mult), "o", u)

            def logits(u):
                b, h = UN[u]
                L = P * (b + 1)
                near = min(L, 256)
                v.wait_ge(lg_full, u + 1)
                v.wait_ge(near_done, u + 1)
                if u >= 2:
                    v.wait_ge(pr_done, u - 1)
                c = u % 4
                if L > near:
                    link(v.tensor_tensor_reduce(nlg[u % 2][:, 0:L - near], lgt[u % 2][:, 0:L - near],
                                                SC[:, SCAT[b]:SCAT[b] + L - near], -1.0, 3e38, ALU.add, ALU.min,
                                                mxa[:, c:c + 1]))
                ini = mxa[:, c:c + 1] if L > near else 3e38
                link(v.tensor_tensor_reduce(nlg[u % 2][:, L - near:L], lgt[u % 2][:, L - near:L],
                                            nearm[c][:, 256 - near:256], -1.0, ini, ALU.add, ALU.min,
                                            nmx[:, c:c + 1]))
                v.sem_inc(mx_done, 1)
                v.sem_inc(lg_used, 1)

            logits(0)
            for u, (b, h) in enumerate(UN):
                if u + 1 < len(UN):
                    logits(u + 1)
                if u >= 1:
                    norm_head(u - 1)
                if b >= 1 and 1 <= h <= 6:
                    mask_step(b - 1, h - 1)
                k = min(b + 1, 4)
                wait_full(v, "pt", u, 0)
                if u >= 2:
                    wait_full(v, "o", u - 2)
                evacuates(v.tensor_copy(pT[u % 2][:, 0:k, :], bank("pt", u, 0)[:, 0:k * P].rearrange(
                    "p (a b) -> p a b", b=P)), "pt", u, 0)
            norm_head(len(UN) - 1)

            wait_full(v, "ot", NTP - 1)
            link(v.memset(qbS, 0.0))
            link(v.memset(relt[0:NB], 0.0))
            q5 = qbS.rearrange("p (b f) (h t) -> p b f h t", f=4, t=DT)
            for f in range(4):
                for e in range(2):
                    src = qdT[64 * e:64 * e + 64, f, SEQ:T].rearrange("p (b t) -> p b t", t=DT)
                    ins = v.tensor_copy(q5[64 * e:64 * e + 64, :, f, 2 * f + e, :], src)
            link(ins)
            v.sem_inc(qbs_done, 1)
            r4 = relt.rearrange("p t (j h u) -> p t j h u", j=4, u=DT)
            for t in range(DT):
                for j in range(4):
                    ins = v.tensor_copy(r4[0:NB, t, j, :, t], relb[0:NB, :])
            link(ins)
            v.sem_inc(relt_done, 1)
            for g in range(2):
                v.wait_ge(so_used, 4 * (g + 1))
                wait_evac(v, "mb", g)
                v.tensor_tensor_reduce(nlS[g], lgt[g][:, 0:NKS], mbS[g], -1.0, 3e38, ALU.add, ALU.min,
                                       nmx[:, g:g + 1]).then_inc(smx, 1)
            for g in range(2):
                v.wait_ge(spr, g + 1)
                if g == 1:
                    wait_full(v, "sl", 0)
                pb_ = k128["pick_b"][:, g * DB:(g + 1) * DB].unsqueeze(2).to_broadcast([P, DB, DT])
                v.tensor_tensor(pnS, prS[g][:, PAST:NKS].unsqueeze(1).to_broadcast([P, DB, DT]), pb_,
                                ALU.mult).then_inc(spn, 1)
                link(v.reciprocal(rrec[:, g:g + 1], rsum[:, g:g + 1]))
                wait_full(v, "so", g)
                if g == 1:
                    wait_full(v, "sot", 0)
                evacuates(v.scalar_tensor_tensor(
                    omS.rearrange("p (h d) -> p h d", h=DH), bank("so", g).rearrange("p (h d) -> p h d", h=DH),
                    rrec[:, g:g + 1], k128["pick_h"].unsqueeze(2).to_broadcast([P, DH, DHD]),
                    ALU.mult, ALU.mult), "so", g)

            v.wait_ge(sp_done, 1)
            for b_ in atb:
                link(v.memset(b_, 0.0))
            ngr = 0
            c64 = lambda t_: t_[:, 0:SEQ].rearrange("p (c s) -> p c s", s=64)
            c128_ = lambda t_: t_[:, 0:SEQ].rearrange("p (c s) -> p c s", s=P)
            c4 = lambda t_: t_[:, SEQ:T].rearrange("p (c s) -> p c s", s=DT)
            QS = float(GDK) ** -0.5
            v.wait_ge(zeroed, 4)
            for h in range(GH):
                for n in range(3):
                    wait_evac(v, "gq", h, n)
                    wait_evac(v, "gk", h, n)
                    wait_evac(v, "gz", h, n)
                v.wait_ge(sp_done, h + 1)
                link(v.scalar_tensor_tensor(uT, uT, 0.0, eT, ALU.min, ALU.subtract))
                link(v.tensor_tensor_scan(Bc, rst, uT, 0.0, ALU.mult, ALU.add))
                if h >= 1:
                    wait_full(v, "gt", h - 1, NTP)
                mid = c64(Bc)[:, :, 31:32].to_broadcast([P, 16, 64])
                link(v.tensor_tensor(c64(dT), c64(Bc), mid, ALU.subtract))
                link(v.tensor_copy(dT[:, SEQ:T], Bc[:, SEQ:T]))
                v.sem_inc(d_done, 2)

                def product(m, dst, q, part=None):
                    v.wait_ge(e_done, 5 * h + m + 1)
                    pick = part or (lambda t_: t_)
                    if q:
                        ins = v.scalar_tensor_tensor(pick(dst), pick(qh), QS, pick(eT), ALU.mult, ALU.mult)
                    else:
                        ins = v.tensor_tensor(pick(dst), pick(kh), pick(eT), ALU.mult)
                    return ins

                link(product(0, Q1, True))
                v.sem_inc(f_done, 1)
                link(product(1, K1, False))
                link(v.tensor_tensor(c128_(dT), c128_(Bc), c128_(Bc)[:, :, 63:64].to_broadcast([P, 8, P]),
                                     ALU.subtract))
                v.sem_inc(d_done, 1)
                v.sem_inc(f_done, 1)
                link(product(2, QK2, False, lambda t_: c128_(t_)[:, :, 0:64]))
                link(product(2, QK2, True, lambda t_: c128_(t_)[:, :, 64:P]))
                link(v.tensor_tensor(c128_(dT), c128_(Bc), c128_(Bc)[:, :, P - 1:P].to_broadcast([P, 8, P]),
                                     ALU.subtract))
                link(v.tensor_tensor(c4(dT), c4(Bc), c4(Bc)[:, :, DT - 1:DT].to_broadcast([P, DB, DT]),
                                     ALU.subtract))
                v.sem_inc(d_done, 2)
                v.sem_inc(f_done, 1)
                link(product(3, Q3, True))
                link(v.tensor_copy(ebl[:, 0:NTP], c128_(eT)[:, :, P - 1]))
                link(v.tensor_copy(ebl[:, NTP:NTP + DB], c4(eT)[:, :, DT - 1]))
                v.sem_inc(f_done, 1)
                link(product(4, K4, False))
                v.sem_inc(f_done, 1)
                link(v.tensor_tensor(q3p, Q3[:, SEQ:T].unsqueeze(1).to_broadcast([P, DB, NS]),
                                     k128["cols_b"].rearrange("p (a b) -> p a b", a=DB), ALU.mult))
                v.sem_inc(q3p_done, 1)
                for f in range(2):
                    for n in range(3):
                        v.wait_ge(sg_done, ngr + 1)
                        evacuates(v.scalar_tensor_tensor(rh[:, f, n * W3:(n + 1) * W3], bank("gr", h, f, n)[:, 0:W3],
                                                         vec[:, 20 + f:21 + f], sig[ngr % 2], ALU.mult, ALU.mult),
                                  "gr", h, f, n)
                        ngr += 1
                def mask_pairs(i):
                    wait_full(v, "at", h, i)
                    bk = bank("at", h, i)
                    if i == NTP:
                        evacuates(v.tensor_tensor(atS[0:NS, :], bk[0:NS, 0:NS], k32["same"], ALU.mult), "at", h, i)
                        return
                    if i >= 2:
                        wait_full(v, "go", h, i - 2)
                    v.tensor_tensor(atb[i % 2][0:64, :], bk[0:64, 0:P], k128["causal"][0:64, :], ALU.mult)
                    evacuates(v.tensor_tensor(atb[i % 2][64:P, 64:P], bk[64:P, 64:P], k128["causal"][64:P, 64:P],
                                              ALU.mult), "at", h, i)

                mask_pairs(0)
                for i in range(NTP):
                    mask_pairs(i + 1)
                    wait_full(v, "ds", h, i)
                    wait_full(v, "go", h, i)
                    if i == 0:
                        if h >= 1:
                            v.wait_ge(st_out, 16 * 2 * h)
                        ins = v.tensor_copy(Sp, bank("ds", h, i)[:, 0:GDV])
                    else:
                        ins = v.scalar_tensor_tensor(Sp, Sp, ebl[:, i:i + 1], bank("ds", h, i)[:, 0:GDV],
                                                     ALU.mult, ALU.add)
                    evacuates(ins, "ds", h, i)
                    wait_evac(v, "ds", h, i)
                v.sem_inc(core_done, 1)
                wait_evac(v, "k4", h, NTP)
                link(v.tensor_tensor(k4p[0:NS], k4T[0][0:NS, :].unsqueeze(1).to_broadcast([NS, DB, P]),
                                     k32["rows_b"].unsqueeze(2).to_broadcast([NS, DB, P]), ALU.mult))
                v.sem_inc(k4p_done, 1)
                wait_full(v, "go", h, NTP)
                for b in range(DB):
                    wait_full(v, "ds", h, NTP + b)
                    evacuates(v.scalar_tensor_tensor(S0[:, b, :], S0[:, b, :], ebl[:, NTP + b:NTP + b + 1],
                                                     bank("ds", h, NTP + b)[:, 0:GDV], ALU.mult, ALU.add),
                              "ds", h, NTP + b)
                for b in range(DB):
                    wait_evac(v, "ds", h, NTP + b)
                v.sem_inc(core_done, 1)
                v.wait_ge(oss_done, h + 1)
                link(v.tensor_scalar(oms, oss, 1.0 / GDV, EPS, ALU.mult, ALU.add))
                v.sem_inc(oms_done, 1)
                v.wait_ge(ort_done, h + 1)
                link(v.reciprocal(ors, ort))
                for i in range(NT + 2):
                    if i < NT:
                        r = rows(i)
                        row = vh[:, i, :] if i < NTP else o8[0:r, :]
                        v.tensor_scalar(row, row, ors[0:r, i:i + 1], None, ALU.mult).then_inc(on_done, 1)
                    if i >= 2:
                        k = i - 2
                        r = rows(k)
                        wait_full(v, "gt", h, k)
                        src = bank("gt", h, k)[:, 0:2 * P].rearrange("p (a b) -> p a b", a=2)[:, :, 0:r]
                        evacuates(v.tensor_tensor(ogT[:, 2 * h:2 * h + 2, k * P:k * P + r], src,
                                                  rh[:, :, k * P:k * P + r], ALU.mult), "gt", h, k)

            m = 0
            for f in range(KD):
                for n in range(3):
                    t1, t2 = msg[4], msg[5]
                    wait_full(v, "my", f, n)
                    wait_evac(v, "mg", f, n)
                    evacuates(v.tensor_tensor(t1, bank("my", f, n)[:, 0:W3], msg[2 * (m % 2)], ALU.mult), "my", f, n)
                    wait_full(v, "mz", f, n)
                    wait_evac(v, "me", f, n)
                    evacuates(v.tensor_tensor(t2, bank("mz", f, n)[:, 0:W3], msg[2 * (m % 2) + 1], ALU.mult),
                              "mz", f, n)
                    wait_evac(v, "my", f, n)
                    wait_evac(v, "mz", f, n)
                    v.tensor_tensor(zT[:, f, n * W3:(n + 1) * W3], t1, t2, ALU.add).then_inc(m_b, 1)
                    m += 1
                    v.wait_ge(m_b, m)
            v.wait_ge(st_out, 32 * GH)
            for i in range(NT + 2):
                if i < NT:
                    r = rows(i)
                    v.wait_ge(r_landed[i % 4], 16 * (i // 4 + 1))
                    for s in range(2):
                        wait_full(v, "wo", i, s)
                        evacuates(v.tensor_tensor(x2[0:r, i, 512 * s:512 * s + 512], bank("wo", i, s)[0:r, :],
                                                  xr[i % 4][0:r, 512 * s:512 * s + 512], ALU.add), "wo", i, s)
                        wait_evac(v, "wo", i, s)
                        v.sem_inc(r_used, 1)
                if 1 <= i <= NT:
                    mean_tile(i - 1, y_sq, y_ms)
                    norm_tile(i - 1, x2[:, i - 1, :], h2[(i - 1) % 2], y_rt, y_h)
                if i >= 2:
                    turn_tile(i - 2, vec[:, 8:16], "h2", hT)
            for m in range(3 * KF):
                f, n = m // 3, m % 3
                v.wait_ge(f_sig, m + 1)
                evacuates(v.tensor_tensor(ft[m % 2], bank("fg", f, n)[:, 0:W3], fsig[m % 2], ALU.mult), "fg", f, n)
                wait_evac(v, "fg", f, n)
                v.sem_inc(f_t, 1)
                wait_full(v, "fu", f, n)
                evacuates(v.tensor_tensor(actT[:, f, n * W3:(n + 1) * W3], bank("fu", f, n)[:, 0:W3], ft[m % 2],
                                          ALU.mult), "fu", f, n)
            v.wait_ge(g_landed, 16)
            for i in range(NT + 1):
                if i < NT:
                    r = rows(i)
                    for c in range(2):
                        wait_full(v, "yt", i, c)
                        evacuates(v.tensor_tensor(x2[0:r, i, 512 * c:512 * c + 512], bank("yt", i, c)[0:r, :],
                                                  x2[0:r, i, 512 * c:512 * c + 512], ALU.add), "yt", i, c)
                    for c in range(2):
                        wait_evac(v, "yt", i, c)
                    v.sem_inc(z_x, 1)
                if i >= 1:
                    r = rows(i - 1)
                    v.wait_ge(z_rt, i)
                    link(v.reciprocal(rstd[0:r, i - 1:i], rt[0:r, i - 1:i]))
                    v.scalar_tensor_tensor(yo[(i - 1) % 3][0:r, :], x2[0:r, i - 1, :], rstd[0:r, i - 1:i], gfb[0:r, :],
                                           ALU.mult, ALU.mult).then_inc(z_o, 1)
                if i < NT:
                    mean_tile(i, z_sq, z_ms)

        @block.gpsimd
        def _(g):
            n_out = 0
            g.memset(kw[:, NTP, :], 0.0).then_inc(zeroed, 1)
            g.memset(qiS, 0.0).then_inc(zeroed, 1)
            g.memset(scs, 0.0).then_inc(zeroed, 1)
            g.wait_ge(c_landed, 16 * N_CONST)
            for n in range(DB * NPG):
                pg = g.value_load(pagetab[0:1, n:n + 1], min_val=0, max_val=a["cache_kidx"].shape[1] - 1)
                src = a["cache_kidx"][0, bass.ds(pg, 1)].rearrange("a s d -> (a s) d")
                for e in range(2):
                    g.dma_start(kpg[:, n, e * IDM:(e + 1) * IDM], src).then_inc(pg_landed, 16)
            for h in range(DH):
                wait_evac(g, "nb", h)
                g.dma_start(scr[h].rearrange("(p c) -> p c", c=384)[:, 0:383], nbs[h % 2]).then_inc(nb_out[h % 2], 16)
            all_nb_out(g)
            for h in range(DH):
                src = scr[h][127:127 + P * 383].rearrange("(p c) -> p c", c=383)[:, 0:256]
                g.dma_start(nearb[:, h, :], src).then_inc(nb_in, 16)
            g.wait_ge(kn_done, 1)
            g.dma_start(o["kidx_p"].rearrange("(i p) d -> p i d", p=P), kn[:, 0:NTP, 0:IDM]).then_inc(ki_out, 16)
            g.dma_start(o["kidx_s"], kn[0:NS, NTP, 0:IDM]).then_inc(ki_out, 16)
            for k, b in enumerate(range(2, NTP)):
                g.wait_ge(sc_done, k + 1)
                d = SC[:, SCAT[b] + b * P:SCAT[b] + (b + 1) * P]
                g.affine_select(out=d, in_=d, compare_op=ALU.is_ge, fill=NEG, base=0, pattern=[[-1, P]],
                                channel_multiplier=1).then_inc(sc_diag, 1)
            for i in range(NT):
                wait_evac(g, "kt", i)
                dst = o["k_p"][i * P:(i + 1) * P, :] if i < NTP else o["k_s"]
                g.dma_start(dst, kst[i % 2][0:rows(i), :]).then_inc(kt_out[i % 2], 16)
            for i in range(NT):
                wait_evac(g, "vd", i)
            g.dma_start(o["v_p"].rearrange("(i p) d -> p i d", p=P), vd[:, 0:NTP, :]).then_inc(outs, 16)
            g.dma_start(o["v_s"], vd[0:NS, NTP, :]).then_inc(outs, 16)
            g.wait_ge(nb_in, 16 * DH)
            g.wait_ge(ki_out, 32)
            all_kt_out(g)
            g.memset(nearz, 0.0).then_inc(pool_seq, 1)
            g.wait_ge(pool_seq, 1)
            g.affine_select(out=nearz[:, P:], in_=nearz[:, P:], compare_op=ALU.is_ge, fill=NEG, base=0,
                            pattern=[[-1, P]], channel_multiplier=1).then_inc(pool_seq, 1)
            g.wait_ge(pool_seq, 2)
            for u, (b, h) in enumerate(UN):
                if u >= 4:
                    g.wait_ge(lg_used, u - 3)
                if b >= 2 and h == 0:
                    g.wait_ge(mask_done, b - 1)
                L = P * (b + 1)
                m = SC[:, SCAT[b] + L - 256:SCAT[b] + L] if b >= 2 else nearz
                g.tensor_tensor(nearm[u % 4], m, nearb[:, h, :], ALU.add).then_inc(near_done, 1)
            def page(b, p, names):
                n = b * NPG + p
                pg = g.value_load(pagetab[0:1, n:n + 1], min_val=0, max_val=a["cache_k"].shape[1] - 1)
                for name, dst, s_ in names:
                    g.dma_start(dst[:, p, :], a[name][0, bass.ds(pg, 1)].rearrange("a s h d -> (a s) (h d)"))\
                     .then_inc(s_, 16)

            g.wait_ge(lg_used, DH * (NTP - 1))
            for b in range(2):
                for p in range(NPG):
                    page(b, p, [("cache_k", kpS[b % 2], ks_landed[b % 2])])
            g.wait_ge(pr_done, len(UN))
            wait_full(g, "o", len(UN) - 1)
            wait_evac(g, "ot", NTP - 1)
            for b in range(4):
                for p in range(NPG):
                    page(b, p, [("cache_v", vpS[b], vs_landed)])
            for b in range(2, DB):
                wait_full(g, "kp", (b - 2) // 4, (b - 2) % 4, 1)
                for p in range(NPG):
                    page(b, p, [("cache_k", kpS[b % 2], ks_landed[b % 2])])
            wait_full(g, "so", 0)
            for b in range(4, DB):
                for p in range(NPG):
                    page(b, p, [("cache_v", vpS[b % 4], vs_landed)])
            wait_evac(g, "sot", 1)
            g.memset(rst, 1.0).then_inc(pool_seq, 1)
            g.wait_ge(pool_seq, 3)
            g.memset(rst[:, 0:SEQ].rearrange("p (c s) -> p c s", s=P)[:, :, 0:1], 0.0).then_inc(pool_seq, 1)
            g.memset(rst[:, SEQ:T].rearrange("p (c s) -> p c s", s=DT)[:, :, 0:1], 0.0).then_inc(zeroed, 1)
            g.dma_start(wgu[0:RANK, :], a["w_gate_up"][0]).then_inc(wgu_in, 16)
            for h in range(GH):
                if h >= 1:
                    g.wait_ge(st_out, 32 * h)
                g.dma_start(S0, a["state_gla"][0, :, h].rearrange("b k v -> k b v")).then_inc(st_in, 16)
                g.wait_ge(core_done, 2 * h + 1)
                g.dma_start(o["gla_p"][h], Sp).then_inc(st_out, 16)
                g.wait_ge(core_done, 2 * h + 2)
                g.dma_start(o["gla_s"][:, h].rearrange("b k v -> k b v"), S0).then_inc(st_out, 16)
            for n in range(3):
                wait_full(g, "dn", KD - 1, n)
            g.dma_start(gfb, a["g_final"].rearrange("(o n) -> o n", o=1).to_broadcast([P, D])).then_inc(g_landed, 16)
            for i in range(NT):
                g.wait_ge(z_o, i + 1)
                dst = o["y_p"][i * P:(i + 1) * P, :] if i < NTP else o["y_s"]
                g.dma_start(dst, yo[i % 3][0:rows(i), :]).then_inc(z_out[i % 3], 16)
            g.wait_ge(outs, 32)
            g.wait_ge(st_out, 32 * GH)
            all_kt_out(g)
            for k in range(3):
                g.wait_ge(z_out[k], 16 * 3)


def kernel(**inputs):
    import concourse.bacc as bacc
    from concourse.bass_utils import run_bass_kernel_spmd

    c128, c32, bits = constants()
    at128, _ = widths(c128)
    at32, _ = widths(c32)
    arrays = {k: np.ascontiguousarray(v) for k, v in inputs.items()}
    arrays["c128"] = np.concatenate(list(c128.values()), 1)
    arrays["c32"] = np.concatenate(list(c32.values()), 1)
    arrays["cbits"] = bits
    nc = bacc.Bacc("TRN2", target_bir_lowering=False, num_devices=1)
    a = {k: nc.dram_tensor(k, v.shape, mybir.dt.from_np(v.dtype), kind="ExternalInput").ap()
         for k, v in arrays.items()}
    shapes = {"y_p": [SEQ, D], "y_s": [NS, D], "k_p": [SEQ, DW], "v_p": [SEQ, DW], "kidx_p": [SEQ, IDM],
              "gla_p": [GH, GDK, GDV], "k_s": [NS, DW], "v_s": [NS, DW], "kidx_s": [NS, IDM],
              "gla_s": [DB, GH, GDK, GDV]}
    o = {k: nc.dram_tensor("out_" + k, s, F32, kind="ExternalOutput").ap() for k, s in shapes.items()}
    build(nc, a, o, at128, at32)
    r = run_bass_kernel_spmd(nc, [arrays], core_ids=[0]).results[0]
    g = {k: r["out_" + k] for k in shapes}
    return (g["y_p"].reshape(1, SEQ, D), g["y_s"].reshape(DB, DT, D),
            g["k_p"].reshape(1, 1, SEQ, DH, DHD), g["v_p"].reshape(1, 1, SEQ, DH, DHD),
            g["kidx_p"].reshape(1, 1, SEQ, IDM), g["gla_p"].reshape(1, 1, GH, GDK, GDV),
            g["k_s"].reshape(1, DB, DT, DH, DHD), g["v_s"].reshape(1, DB, DT, DH, DHD),
            g["kidx_s"].reshape(1, DB, DT, IDM), g["gla_s"].reshape(1, DB, GH, GDK, GDV))
```

```python
from contextlib import ExitStack

import numpy as np

import concourse.bass as bass
from concourse import mybir

F32 = mybir.dt.float32
F32R = mybir.dt.float32r
I32 = mybir.dt.int32
ALU = mybir.AluOpType
ACT = mybir.ActivationFunctionType
X = mybir.AxisListType.X

P = 128
D = 1024
SEQ = 1024
DB, DT = 8, 4
NS = DB * DT
T = SEQ + NS
NTP = SEQ // P
NT = NTP + 1
KD = D // P
PAST, PAGE = 256, 128
NPG = PAST // PAGE
NKS = PAST + DT
GH, GDK, GDV = 4, 128, 256
RANK = 16
DH, DHD = 8, 64
DW = DH * DHD
IH, IDM = 4, 64
TOPK = 256
TOPK_S = NKS // 4
DFF = 2816
KF = DFF // P
NB = 32
EPS = 1e-6
NEG = -1e30
SPLITS = dict(qg=512, kg=512, vg=1024, rg=1024, al=RANK, qd=DW, kd=DW, vd=DW, qi=IH * IDM,
              ki=IDM, wi=IH, gg=D, gd=D)
COL, _at = {}, 0
for _name, _w in SPLITS.items():
    COL[_name] = _at
    _at += _w
DIN = _at
W3 = T // 3
TCH = [(n * W3, W3) for n in range(3)]
OHW = 387


def rows(i):
    return P if i < NTP else NS


def constants():
    r = np.arange(P)
    j, q = r // 32, r % 32
    h, t = q // 4, q % 4
    tok_b, tok_t = np.arange(NS) // DT, np.arange(NS) % DT
    own = lambda g: (tok_b[:, None] == 4 * g + j[None]) & (tok_t[:, None] == t[None])
    exp_i = np.stack([own(g) & (h < IH)[None] for g in range(2)], 1)
    exp_h = np.stack([own(g) for g in range(2)], 1)
    n = np.maximum(259 - np.arange(OHW), 0)
    half = NB // 2
    large = half + (np.log(np.maximum(n, 1).astype(np.float32) / np.float32(half))
                    / np.float32(np.log(128 / half)) * np.float32(NB - half)).astype(np.int32)
    bucket = np.where(n < half, n, np.minimum(large, NB - 1))
    onehot = np.arange(NB)[:, None] == bucket[None]
    f = lambda a: np.ascontiguousarray(np.asarray(a, np.float32).reshape(a.shape[0], -1))
    s, c = np.arange(P), np.arange(P)
    c128 = {
        "ident": f(np.eye(P)),
        "causal": f(c[None] >= s[:, None]),
        "sum_i": f(np.transpose(exp_i, (2, 1, 0))),
        "pick_i": f((h[:, None] == np.arange(IH)[None])),
        "pick_h": f((h[:, None] == np.arange(DH)[None])),
        "pick_b": f(np.stack([(4 * g + j)[:, None] == np.arange(DB)[None] for g in range(2)], 1)),
        "sum_t": f((j[:, None] == np.arange(16)[None] // 4) & (t[:, None] == np.arange(16)[None] % 4)),
        "cols_b": f(np.broadcast_to(np.arange(NS)[None, None] // DT == np.arange(DB)[None, :, None],
                                    (P, DB, NS))),
        "bits_f": f(np.broadcast_to(np.append(2.0 ** np.arange(30, -1, -1), 0.0), (P, 32))),
    }
    future = tok_t[:, None] < np.arange(DT)[None]
    c32 = {
        "exp_i": f(exp_i), "exp_h": f(exp_h), "onehot": f(onehot),
        "same": f((tok_b[:, None] == tok_b[None]) & (tok_t[:, None] <= tok_t[None])),
        "future": f(np.where(future, NEG, 0.0)),
        "rows_b": f(tok_b[:, None] == np.arange(DB)[None]),
    }
    bits = np.broadcast_to(np.append(1 << np.arange(30, -1, -1), 0).astype(np.int32), (P, 32))
    return c128, c32, np.ascontiguousarray(bits)


def widths(table):
    out, at = {}, 0
    for k, v in table.items():
        out[k] = (at, v.shape[1])
        at += v.shape[1]
    return out, at


def build(nc, a, o, c128_at, c32_at):
    ctx = ExitStack()
    with ctx:
        sem = lambda n: ctx.enter_context(nc.semaphore(n))
        n128, n32 = sum(w for _, w in c128_at.values()), sum(w for _, w in c32_at.values())

        ARENA = 53200
        arena = ctx.enter_context(nc.sbuf_tensor("arena", [P, ARENA], F32))
        arena_at = nc.sbuf_base - 4 * ARENA
        top = [0]

        def region(n):
            at = top[0]
            top[0] += n
            assert top[0] <= ARENA, top[0]
            return at

        def at(off, *shape):
            n = int(np.prod(shape))
            v = arena[:, off:off + n]
            if len(shape) == 2:
                v = v.rearrange("p (a b) -> p a b", a=shape[0])
            if len(shape) == 3:
                v = v.rearrange("p (a b c) -> p a b c", a=shape[0], b=shape[1])
            return v

        o_c128, o_c32 = region(n128), region(n32)
        k128 = {k: arena[:, o_c128 + s:o_c128 + s + w] for k, (s, w) in c128_at.items()}
        k32 = {k: arena[0:32, o_c32 + s:o_c32 + s + w] for k, (s, w) in c32_at.items()}
        ident = k128["ident"]
        small = region(421)
        o_hT = region(KD * T)
        o_w = region(2 * 4096)
        base = top[0]

        hT = at(o_hT, KD, T)
        wslot = [arena[:, o_w + s * 4096:o_w + (s + 1) * 4096] for s in range(2)]

        s_at = [small]

        def tiny(n, dt=F32):
            v = arena[:, s_at[0]:s_at[0] + n]
            s_at[0] += n
            assert s_at[0] <= small + 420
            return v if dt == F32 else v.bitcast(dt)

        vec = tiny(22)
        ssq, msq, rt, rstd = tiny(NT), tiny(NT), tiny(NT), tiny(NT)
        one = tiny(1)
        kmu, kvar, krt, krs = tiny(NT), tiny(NT), tiny(NT), tiny(NT)
        cnt, need = tiny(7), tiny(7)
        thr, gbit = tiny(7, I32), tiny(7, I32)
        cand = tiny(7, I32)
        bits = tiny(32, I32)
        wrow = tiny(2)
        wtmp = tiny(4)
        mxa, mxb, nmx, rsum, rrec = tiny(4), tiny(4), tiny(4), tiny(4), tiny(4)
        ebl = tiny(NTP + DB)
        relb = tiny(DH)
        r31 = tiny(DH)
        pagetab = tiny(16, I32)
        oss, oms, ort, ors = tiny(NT), tiny(NT), tiny(NT), tiny(NT)

        ring = ctx.enter_context(nc.psum_tensor("ring", [P, 4, 512], F32))
        lgt = [ctx.enter_context(nc.psum_tensor(f"lgt{i}", [P, 1024], F32)) for i in range(2)]
        full = [sem(f"full{i}") for i in range(4)]
        evac = [sem(f"evac{i}") for i in range(4)]
        ready = [0]
        chunk = {}

        def plan(*key):
            chunk[key] = ready[0]
            ready[0] += 1

        plan("vec")
        for i in range(NT):
            plan("h", i, 0), plan("h", i, 1)
        for h in range(DH):
            plan("nb", h)
        for f in range(2):
            for n in range(3):
                plan("qi", f, n)
        for i in range(NT):
            plan("ki", i)
        for n in range(3):
            plan("al", n)
        for n in range(3):
            plan("kiT", n)
        for n in range(4):
            plan("ps", n)
        SCC = [(b, h, c0, min(512, P * (b + 1) - c0)) for b in range(2, NTP)
               for c0 in range(0, P * (b + 1), 512) for h in range(IH)]
        for k in SCC:
            plan("sc", *k)
        for g in range(2):
            plan("wr", g), plan("si", g)
        plan("ss")
        for w in ("qd", "kd"):
            for f in range(4):
                for n in range(3):
                    plan(w, f, n)
        for i in range(NT):
            plan("kt", i)
        for i in range(NT):
            plan("vd", i)
        UN = [(b, h) for b in range(NTP) for h in range(DH)]
        for u in range(len(UN) + 1):
            if u >= 1:
                plan("o", u - 1)
                if u % DH == 0:
                    plan("ot", u // DH - 1)
            if u < len(UN):
                for c in range((UN[u][0] + 4) // 4):
                    plan("pt", u, c)
        for g in range(2):
            for j in range(4):
                for p in range(NPG):
                    plan("kp", g, j, p)
            plan("mb", g)
        for w in ("gq", "gk"):
            for n in range(3):
                plan(w, 0, n)
        for g in range(2):
            plan("sl", g), plan("spt", g), plan("so", g), plan("sot", g)
        for h in range(GH):
            for w in ("gq", "gk"):
                for n in range(3):
                    if h:
                        plan(w, h, n)
            if h >= 1:
                for i in range(NT):
                    plan("gt", h - 1, i)
            for n in range(3):
                plan("gz", h, n)
            for i in range(NT):
                plan("gv", h, i)
            for f in range(2):
                for n in range(3):
                    plan("gr", h, f, n)
            plan("at", h, 0), plan("k4", h, 0)
            for i in range(NTP):
                plan("at", h, i + 1), plan("k4", h, i + 1)
                plan("go", h, i), plan("ds", h, i)
            plan("go", h, NTP)
            for b in range(DB):
                plan("ds", h, NTP + b)
        plan("me", 0, 0)
        for i in range(NT):
            plan("gt", GH - 1, i)
        ROUNDS_M = [("me", "mz", f) for f in range(KD)] + [("mg", "my", f) for f in range(KD)]
        for q, (gate, branch, f) in enumerate(ROUNDS_M):
            for n in range(3):
                if q or n:
                    plan(gate, f, n)
            for n in range(3):
                plan(branch, f, n)
        for i in range(NT):
            plan("wo", i, 0), plan("wo", i, 1)
            if i >= 2:
                plan("h2", i - 2, 0), plan("h2", i - 2, 1)
        for i in (NT - 2, NT - 1):
            plan("h2", i, 0), plan("h2", i, 1)
        for half in range(2):
            for f in range(2):
                for n in range(3):
                    plan("fg", half, f, n), plan("fu", half, f, n)
            for i in range(NT):
                plan("dn", half, i, 0), plan("dn", half, i, 1)
        PAIR = 2 * (12 + 2 * NT) // 4
        assert 4 * PAIR == 2 * (12 + 2 * NT)

        def bank(*key):
            return ring[:, chunk[key] % 4, :]

        def wait_full(eng, *key, more=0):
            eng.wait_ge(full[chunk[key] % 4], more + (chunk[key] // 4 + 1))

        def wait_evac(eng, *key, more=0):
            eng.wait_ge(evac[chunk[key] % 4], more + (chunk[key] // 4 + 1))

        def evacuates(ins, *key):
            return ins.then_inc(evac[chunk[key] % 4], 1)

        def wsrc(name, c0, n, k=KD):
            return a[name].rearrange("l (k p) n -> p (l k) n", p=P)[:, 0:k, c0:c0 + n]

        units = [("idx", [("w_in", COL["qi"], 324, 0), ("w_in", COL["al"], RANK, 324)], 340, KD)]
        for w in ("qd", "kd", "vd"):
            units.append((w, [("w_in", COL[w], 512, 0)], 512, KD))
        for s in range(2):
            units.append((("wo", s), [("w_o", 512 * s, 512, 0)], 512, KD))
        unit_no = {u[0]: n for n, u in enumerate(units)}
        w_landed = [sem(f"w_landed{s}") for s in range(2)]
        last_chunk = {"idx": ("al", 2), "qd": ("qd", 3, 2), "kd": ("kd", 3, 2), "vd": ("vd", NTP),
                      ("wo", 0): ("wo", NTP, 0), ("wo", 1): ("wo", NTP, 1)}
        w_count = []
        per = [0, 0]
        for n, (_, parts, _, _) in enumerate(units):
            per[n % 2] += len(parts)
            w_count.append(16 * per[n % 2])

        def wview(name):
            n = unit_no[name]
            _, parts, w, k = units[n]
            return wslot[n % 2][:, 0:k * w].rearrange("p (k n) -> p k n", n=w)

        def wait_w(eng, name):
            n = unit_no[name]
            eng.wait_ge(w_landed[n % 2], w_count[n])

        top[0] = base
        o_SC = region(4484)
        o_alT = region(T)
        o_odT = region(4 * T)
        SCAT, _n = {}, 0
        for b in range(2, NTP):
            SCAT[b] = _n
            _n += P * (b + 1)
        SC = arena[:, o_SC:o_SC + 4484]
        scs = SC[:, _n:_n + NKS]
        alT = at(o_alT, T)
        odT = at(o_odT, 4, T)
        o_qd = region(4 * T)
        o_kd = region(4 * T)
        region(4)
        o_vd = region(NT * DW)
        o_nb = region(DH * 256)
        o_free = top[0]
        qdT, kdT, vd = at(o_qd, 4, T), at(o_kd, 4, T), at(o_vd, NT, DW)
        nearb = at(o_nb, DH, 256)
        xa = [arena[:, o_qd + i * D:o_qd + (i + 1) * D] for i in range(4)]
        sqj = arena[:, o_kd:o_kd + D]
        relx = at(o_kd + D, DH, P)
        top[0] = o_free
        kw = at(region(NT * 68), NT, 68)
        kn = at(region(NT * P), NT, P)
        kd2 = at(region(NT * IDM), NT, IDM)
        kiT = at(region(T), T)
        qiT = at(region(2 * T), 2, T)
        o_gb = region(2 * IDM)
        kg_b, kb_b = at(o_gb, IDM), at(o_gb + IDM, IDM)
        assert top[0] <= ARENA
        kiS = at(o_odT, DB, PAST)
        qiS = at(o_odT + DB * PAST, DB * 2, 32)
        rl = [arena[:, o_odT + 2560 + i * 512:o_odT + 2560 + (i + 1) * 512] for i in range(2)]
        rs_s = arena[:, o_odT + 3584:o_odT + 3584 + NKS]
        kpg = at(o_vd, 16, P)
        nbs = [arena[:, o_vd + 2048 + i * 384:o_vd + 2048 + i * 384 + 383] for i in range(2)]
        vrow = arena[:, o_vd + 2048 + 768:o_vd + 2048 + 768 + P]
        top[0] = o_free
        nlg = [at(region(1024), 1024) for _ in range(2)]
        pr = [at(region(1024), 1024) for _ in range(2)]
        junk = at(o_free + NT * (68 + P + IDM), 1121).bitcast(mybir.dt.uint8)
        top[0] = o_free + NT * 68 + NT * P + NT * IDM + T + 2 * T + 2 * IDM
        kst = [at(region(DW), DW) for _ in range(2)]
        top[0] = o_free
        nlg = [at(region(1024), 1024) for _ in range(2)]
        pr = [at(region(1024), 1024) for _ in range(2)]
        pT = [at(region(1024), 8, P) for _ in range(2)]
        nearm = [at(region(256), 256) for _ in range(4)]
        osb = [at(region(DW), DW) for _ in range(2)]
        nearz = at(region(256), 256)
        U16 = mybir.dt.uint16
        eqc, inc = at(region(512), 512).bitcast(U16), at(region(512), 512).bitcast(U16)
        kpS = [at(o_SC + 256 + i * NPG * DW, NPG, DW) for i in range(2)]
        top[0] = o_free
        vpS = [at(region(NPG * DW), NPG, DW) for _ in range(4)]
        vpS += [at(o_SC + 256 + 2 * T, NPG, DW), at(region(NPG * DW), NPG, DW), vpS[1], vpS[2]]
        kTs = [at(region(4 * PAST), 4, PAST) for _ in range(2)]
        mbS = [at(region(NKS), NKS) for _ in range(2)]
        nlS = [at(region(NKS), NKS) for _ in range(2)]
        prS = [at(region(NKS), NKS) for _ in range(2)]
        pnS = at(region(NS), DB, DT)
        ptS = at(region(3 * P), 3, P)
        omS = at(region(DW), DW)
        assert top[0] <= ARENA, top[0]
        qbS = at(o_nb, DB * 4, 32)
        relt = at(o_nb + 1024, 4, P)

        def placed(name, dt, off, *shape):
            assert off + int(np.prod(shape)) <= ARENA
            t_ = nc.alloc_sbuf_tensor_at(name, [P, int(np.prod(shape))], dt, offset=arena_at + 4 * off)
            return t_.rearrange("p (a b) -> p a b", a=shape[0]) if len(shape) == 2 else t_[:, :]

        def halves(name, off, *shape):
            return placed(name, F32R, off, *shape)

        n_lo = [halves(f"n_lo{k}", o_hT + k * T, T) for k in range(KD)]
        n_hi = [halves(f"n_hi{k}", o_w + k * T, T) for k in range(KD)]
        mix = o_w + KD * T
        WQ = KD * P
        o_pc = mix + 9512
        praw = [placed(f"piece_whole{i}", F32, o_pc + i * WQ, KD, P) for i in range(2)]
        pw_hi = halves("piece_hi", o_pc + 2 * WQ, 4 * KD, P)
        pw_lo = halves("piece_lo", o_pc + 6 * WQ + 2304, 4 * KD, P)
        pieces = []
        for h in range(GH):
            for k, c0, last in (("qg", GDK * h, ("gq", h, 2)), ("kg", GDK * h, ("gk", h, 2)),
                                ("vg", GDV * h, ("gv", h, NTP)), ("vg", GDV * h + P, ("gv", h, NTP)),
                                ("rg", GDV * h, ("gr", h, 0, 2)), ("rg", GDV * h + P, ("gr", h, 1, 2))):
                pieces.append(("w_in", COL[k] + c0, KD, last))
        M0 = len(pieces)
        for gate, branch, f in ROUNDS_M:
            pieces.append(("w_in", COL["gd" if gate == "me" else "gg"] + P * f, KD, (gate, f, 2)))
            pieces.append(("w_dsa_branch", P * f, 4, (branch, f, 2)) if branch == "mz" else
                          ("w_gla_branch", P * f, KD, (branch, f, 2)))

        def piece(n):
            k, s_ = pieces[n][2], n % 4
            raw = praw[n % 2] if n < M0 + 2 else praw_m
            if n < M0:
                return raw, pw_hi[:, s_ * KD:(s_ + 1) * KD, :], pw_lo[:, s_ * KD:(s_ + 1) * KD, :]
            return raw[:, 0:k, :], pm_hi[s_][:, 0:k, :], pm_lo[s_][:, 0:k, :]

        qh, kh = at(mix, T), at(mix + T, T)
        S0 = at(mix + 2 * T, DB, GDV)
        assert mix + 2 * T + DB * GDV <= o_alT and o_odT + 4 * T <= o_pc
        Q1, K1, QK2, Q3 = (at(o_odT + i * T, T) for i in range(4))
        vh = at(o_pc + 6 * WQ, NT, GDV)
        top[0] = o_pc + 10 * WQ + 2304
        ogs = at(region(2 * T), 2, T)
        Sp = at(region(GDV), GDV)
        atb = [at(region(P), P) for _ in range(2)]
        wgu = at(region(4 * P), 4 * P)
        rh = at(region(2 * T), 2, T)
        o_dT, o_eT = region(T), region(T)
        dT, eT = at(o_dT, T), at(o_eT, T)
        uT, rst, Bc, K4 = (at(region(T), T) for _ in range(4))
        gsq = at(o_dT, GDV)
        q3p = at(o_dT + 256, DB, NS)
        o8 = at(o_dT + 512, GDV)
        atS = at(o_dT + 768, NS)
        k4T = [at(o_dT + 800 + i * P, P) for i in range(2)]
        k4p = at(o_eT, DB, P)
        sig = [Bc[:, i * W3:(i + 1) * W3] for i in range(2)]
        od_hi = halves("od_hi", mix, 4, T)
        od_whole, od_lo = placed("od_whole", F32, mix + 4 * T, 4, T), halves("od_lo", mix + 4 * T, 4, T)
        og_hi = halves("og_hi", mix, KD, T)
        og_whole, og_lo = placed("og_whole", F32, mix + KD * T, KD, T), halves("og_lo", mix + KD * T, KD, T)
        o_zT = mix + 2 * KD * T + 512
        zT = at(o_zT, KD, T)
        o_pm = o_zT + KD * T
        assert o_pm + 8 * WQ <= ARENA
        pm_hi = [halves(f"merge_hi{i}", o_pm + (i ^ 2) * 2 * WQ, KD, P) for i in range(4)]
        pm_lo = [halves(f"merge_lo{i}", o_pm + (i ^ 2) * 2 * WQ + WQ, KD, P) for i in range(4)]
        o_tab = o_c128 + P
        praw_m = placed("merge_whole", F32, o_tab, KD, P)
        msg = [at(o_tab + WQ, W3), at(mix + 2 * KD * T, W3)]
        assert o_tab + WQ + W3 <= small
        top[0] = base
        x2 = at(region(NT * D), NT, D)
        o_hlo = region(KD * T)
        assert o_zT >= top[0]
        o_xr = o_zT + KD * T
        xr = [arena[:, o_xr + i * D:][:, 0:D] for i in range(2)]
        h2 = [arena[:, o_xr + (2 + i) * D:][:, 0:D] for i in range(2)]
        h2t = [placed(f"h_whole{i}", F32, o_tab + i * 4 * P, 4, P) for i in range(2)]
        h_hi, h_lo = halves("h_hi", o_hT, KD, T), halves("h_lo", o_hlo, KD, T)
        FU = 2 * P
        WP = KD * FU
        w_hi = [halves("gate_hi", o_w, KD, FU), halves("up_hi", o_w + 2 * WP, KD, FU)]
        w_lo = [halves("gate_lo", o_w + WP, KD, FU), halves("up_lo", o_w + 3 * WP, KD, FU)]
        a_hi, a_lo = halves("act_hi", top[0], 2, T), halves("act_lo", top[0] + 2 * T, 2, T)
        w_hi.append(halves("down_hi", top[0] + 4 * T, 2, D))
        w_lo.append(halves("down_lo", top[0] + 4 * T + WP, 2, D))
        o_raw = [ARENA - (k + 1) * WP for k in range(3)]
        assert top[0] + 4 * T + 2 * WP <= o_raw[2] and o_raw[0] >= o_xr + 4 * D
        wraw = [placed("gate_whole", F32, o_raw[0], KD, FU), placed("up_whole", F32, o_raw[1], KD, FU),
                placed("down_whole", F32, o_raw[2], 2, D)]
        fsig = [at(o_tab + i * W3, W3) for i in range(2)]
        ft = placed("act_whole", F32, o_tab + 2 * W3, W3)
        assert o_tab + 3 * W3 <= small and o_tab + 8 * P <= small
        gfb = arena[:, o_hT:o_hT + D]
        yo = [arena[:, o_hT + (1 + i) * D:o_hT + (2 + i) * D] for i in range(3)]
        sq_out = lgt[0][:, :]

        od_mem = nc.dram_tensor("dsa_outputs", [P, 4 * T], F32, kind="Internal").ap()
        og_mem = nc.dram_tensor("gla_outputs", [P, KD * T], F32, kind="Internal").ap()
        scr = nc.dram_tensor("near_bias_rows", [DH, P * 384], F32, kind="Internal").ap()

        c_landed = sem("c_landed")
        x_landed = [sem(f"x_landed{i}") for i in range(4)]
        x_used = sem("x_used")
        x_sq, x_ms, x_rt, x_h = sem("x_sq"), sem("x_ms"), sem("x_rt"), sem("x_h")
        relx_done, nb_in = sem("relx_done"), sem("nb_in")
        nb_out = [sem(f"nb_out{i}") for i in range(2)]
        zeroed = sem("zeroed")
        kv_done, krt_done, kn_done = sem("kv_done"), sem("krt_done"), sem("kn_done")
        pg_landed = sem("pg_landed")
        qis_done = sem("qis_done")
        rl_used = sem("rl_used")
        sc_done, sc_diag = sem("sc_done"), sem("sc_diag")
        rsw_done = sem("rsw_done")
        mask_done = sem("mask_done")
        kt_out = [sem(f"kt_out{i}") for i in range(2)]
        ki_out = sem("ki_out")
        outs = sem("outs")
        near_done = sem("near_done")
        lg_full, lg_used = sem("lg_full"), sem("lg_used")
        mx_done, pr_done = sem("mx_done"), sem("pr_done")
        ks_landed = [sem(f"ks_landed{i}") for i in range(2)]
        vs_landed = [sem(f"vs_landed{i}") for i in range(2)]
        qbs_done, relt_done = sem("qbs_done"), sem("relt_done")
        smx, spr, spn = sem("smx"), sem("spr"), sem("spn")
        so_used = sem("so_used")
        wgu_in, st_in, st_out = sem("wgu_in"), sem("st_in"), sem("st_out")
        sp_done = sem("sp_done")
        d_done, e_done, f_done = sem("d_done"), sem("e_done"), sem("f_done")
        sg_done = sem("sg_done")
        q3p_done, k4p_done = sem("q3p_done"), sem("k4p_done")
        oss_done, oms_done, ort_done, on_done = sem("oss_done"), sem("oms_done"), sem("ort_done"), sem("on_done")
        core_done = sem("core_done")
        n_hi_done, n_lo_done = sem("n_hi_done"), sem("n_lo_done")
        p_landed = [sem(f"p_landed{i}") for i in range(2)]
        p_hi_done, p_lo_done = sem("p_hi_done"), sem("p_lo_done")
        od_out, od_landed = sem("od_out"), sem("od_landed")
        og_out, og_landed = sem("og_out"), sem("og_landed")
        od_hi_done, od_lo_done = sem("od_hi_done"), sem("od_lo_done")
        og_hi_done, og_lo_done = sem("og_hi_done"), sem("og_lo_done")
        z_done = sem("z_done")
        r_landed = [sem(f"r_landed{i}") for i in range(2)]
        r_used = sem("r_used")
        y_sq, y_ms, y_rt, y_h = sem("y_sq"), sem("y_ms"), sem("y_rt"), sem("y_h")
        h_hi_done, h_lo_done = sem("h_hi_done"), sem("h_lo_done")
        raw_landed = [sem(f"{k}_landed") for k in ("gate", "up", "down")]
        w_hi_done = [sem(f"{k}_hi_done") for k in ("gate", "up", "down")]
        w_lo_done = [sem(f"{k}_lo_done") for k in ("gate", "up", "down")]
        f_sig, a_hi_done, a_lo_done = sem("f_sig"), sem("a_hi_done"), sem("a_lo_done")
        x2_done = sem("x2_done")
        g_landed = sem("g_landed")
        z_sq, z_ms, z_rt, z_o = sem("z_sq"), sem("z_ms"), sem("z_rt"), sem("z_o")
        z_out = [sem(f"z_out{i}") for i in range(3)]
        act_seq, dve_seq, pool_seq = sem("act_seq"), sem("dve_seq"), sem("pool_seq")

        N_CONST = 11

        def all_nb_out(eng):
            for s_ in nb_out:
                eng.wait_ge(s_, 16 * DH // 2)

        def all_kt_out(eng):
            eng.wait_ge(kt_out[0], 16 * ((NT + 1) // 2))
            eng.wait_ge(kt_out[1], 16 * (NT // 2))

        xp, xs = a["x_prompt"][0], a["x_sample"].rearrange("b t d -> (b t) d")

        def x_src(i):
            return xp[i * P:(i + 1) * P, :] if i < NTP else xs

        block = ctx.enter_context(nc.Block())

        def load_w(sp, n):
            name, parts, w, k = units[n]
            if n >= 2:
                wait_full(sp, *last_chunk[units[n - 2][0]])
            for src, c0, c, d0 in parts:
                sp.dma_start(wview(name)[:, :, d0:d0 + c], wsrc(src, c0, c, k)).then_inc(w_landed[n % 2], 16)

        UNITS = DFF // FU
        PAIRS = UNITS // 2
        assert UNITS == 2 * PAIRS + 1

        def raw_src(k, u):
            if k < 2:
                w = a[("w_ffn_gate", "w_ffn_up")[k]].rearrange("l (k p) n -> p (l k) n", p=P)
                return w[:, :, bass.ds(u * FU, FU)]
            w = a["w_ffn_down"].rearrange("l (k p) n -> p (l k) n", p=P)
            return w[:, bass.ds(u * 2, 2), :]

        @block.sync
        def _(sp):
            def load_raw(k, u):
                sp.dma_start(wraw[k], raw_src(k, u)).then_inc(raw_landed[k], 16)

            sp.dma_start(arena[:, o_c128:o_c128 + n128], a["c128"]).then_inc(c_landed, 16)
            for i in range(NT):
                if i == 3:
                    sp.dma_start(arena[0:32, o_c32:o_c32 + n32], a["c32"]).then_inc(c_landed, 16)
                    sp.dma_start(bits, a["cbits"]).then_inc(c_landed, 16)
                    sp.dma_start(vrow[0:8, :], a["g_mix"].rearrange("l (k p) -> (l k) p", p=P)).then_inc(c_landed, 16)
                    sp.dma_start(vrow[8:16, :], a["g_ffn"].rearrange("l (k p) -> (l k) p", p=P)).then_inc(c_landed, 16)
                    sp.dma_start(vrow[16:20, :], a["b_gate"].rearrange("l (k p) -> (l k) p", p=P)).then_inc(c_landed, 16)
                    sp.dma_start(vrow[20:22, :], a["gla_norm_g"].rearrange("l (k p) -> (l k) p", p=P)).then_inc(c_landed, 16)
                    sp.dma_start(relb[0:NB, :], a["rel_bias"]).then_inc(c_landed, 16)
                    sp.dma_start(kg_b, a["idx_k_g"].to_broadcast([P, IDM])).then_inc(c_landed, 16)
                    sp.dma_start(kb_b, a["idx_k_b"].to_broadcast([P, IDM])).then_inc(c_landed, 16)
                    sp.dma_start(pagetab[0:1, :], a["page_table"].rearrange("(o b) g -> o (b g)", o=1)).then_inc(c_landed, 16)
                    load_w(sp, 0)
                if i >= 4:
                    sp.wait_ge(x_used, i - 3)
                sp.dma_start(xa[i % 4][0:rows(i), :], x_src(i)).then_inc(x_landed[i % 4], 16)
            n_wo = unit_no[("wo", 0)]
            for n in range(1, n_wo):
                load_w(sp, n)
            sp.wait_ge(qbs_done, 1)
            wait_full(sp, "o", len(UN) - 1)
            for n, (src, c0, k, _) in enumerate(pieces):
                if 2 <= n <= M0 + 2:
                    sp.wait_ge(p_lo_done, n - 1)
                if n == M0 + 2:
                    sp.wait_ge(core_done, 2 * GH)
                if n > M0 + 2:
                    sp.wait_ge(p_lo_done, n)
                sp.dma_start(piece(n)[0], wsrc(src, c0, P, k)).then_inc(p_landed[n % 2], 16)
            wait_full(sp, "mg", KD - 1, 2)
            for n in range(n_wo, len(units)):
                load_w(sp, n)
                if n == n_wo + 1:
                    for i in range(NT):
                        if i == 0:
                            sp.wait_ge(z_done, 6 * KD)
                        if i >= 2:
                            sp.wait_ge(r_used, 2 * (i - 1))
                        sp.dma_start(xr[i % 2][0:rows(i), :], x_src(i)).then_inc(r_landed[i % 2], 16)
                        if i == 1:
                            load_raw(0, 0)
                            load_raw(1, 0)
            for c in range(2):
                wait_full(sp, "h2", NT - 2, c)
                wait_full(sp, "h2", NT - 1, c)
            load_raw(2, 0)
            with sp.Fori(0, PAIRS) as i:
                for half in range(2):
                    for k in range(3):
                        src = raw_src(k, i * 2 + (half + 1))
                        sp.wait_ge(w_lo_done[k], i * 2 + (half + 1))
                        sp.dma_start(wraw[k], src).then_inc(raw_landed[k], 16)

        @block.tensor
        def _(pe):
            def begin(*key):
                c = chunk[key]
                if c >= 4:
                    pe.wait_ge(evac[c % 4], c // 4)
                return ring[:, c % 4, :]

            def done(ins, *key):
                ins.then_inc(full[chunk[key] % 4], 1)

            def feature_major(key, w, c0, m, n, src=hT, k=KD):
                ps = begin(*key)
                t0, tn = TCH[n]
                for kk in range(k):
                    ins = pe.matmul(ps[0:m, 0:tn], w[:, kk, c0:c0 + m], src[:, kk, t0:t0 + tn],
                                    start=kk == 0, stop=kk == k - 1)
                done(ins, *key)

            def token_major(key, w, c0, m, i, src=hT, k=KD):
                ps = begin(*key)
                for kk in range(k):
                    ins = pe.matmul(ps[0:rows(i), 0:m], src[:, kk, i * P:i * P + rows(i)], w[:, kk, c0:c0 + m],
                                    start=kk == 0, stop=kk == k - 1)
                done(ins, *key)

            def transposes(key, pairs, m=P):
                ps = begin(*key)
                for c, src in pairs:
                    k = src.shape[0]
                    ins = pe.transpose(ps[0:src.shape[1], c:c + k], src, ident[0:k, 0:k])
                done(ins, *key)

            def three_passes(out, lhi, llo, rhi, rlo, first, last):
                pe.matmul(out, lhi, rhi, start=first, stop=False)
                pe.matmul(out, lhi, rlo, start=False, stop=False)
                return pe.matmul(out, llo, rhi, start=False, stop=last)

            def by_piece(key, np_, n, hi=n_hi, lo=n_lo, split=None):
                pe.wait_ge(p_lo_done, np_ + 1)
                _, w_hi_, w_lo_ = piece(np_)
                ps = begin(*key)
                t0, tn = TCH[n]
                k = pieces[np_][2]
                for kk in range(k):
                    if split is not None:
                        pe.wait_ge(split, kk + 1)
                    ins = three_passes(ps[:, 0:tn], w_hi_[:, kk, :], w_lo_[:, kk, :], hi[kk][:, t0:t0 + tn],
                                       lo[kk][:, t0:t0 + tn], kk == 0, kk == k - 1)
                done(ins, *key)

            pe.wait_ge(c_landed, 16 * N_CONST)
            transposes(("vec",), [(0, vrow[0:22, :])])
            for i in range(NT):
                pe.wait_ge(x_h, i + 1)
                for c in range(2):
                    transposes(("h", i, c), [(P * s, xa[i % 4][0:rows(i), (4 * c + s) * P:(4 * c + s + 1) * P])
                                             for s in range(4)])
            pe.wait_ge(relx_done, 1)
            for h in range(DH):
                ps = begin("nb", h)
                done(pe.matmul(ps[:, 0:383], relx[0:NB, h, :], k32["onehot"][:, 4:OHW], start=True, stop=True),
                     "nb", h)

            for i in range(NT):
                wait_evac(pe, "h", i, 1)
            wait_evac(pe, "h", NT - 1, 0)
            wait_w(pe, "idx")
            w = wview("idx")
            for f in range(2):
                for n in range(3):
                    feature_major(("qi", f, n), w, f * P, P, n)
            for i in range(NT):
                token_major(("ki", i), w, 256, 68, i)
            for n in range(3):
                ps = begin("al", n)
                for kk in range(KD):
                    ins = pe.matmul(ps[0:RANK, 0:W3], w[:, kk, 324:340], hT[:, kk, n * W3:(n + 1) * W3],
                                    start=kk == 0, stop=kk == KD - 1)
                done(ins, "al", n)
            pe.wait_ge(kn_done, 1)
            for n in range(3):
                transposes(("kiT", n), [(P * s, kn[0:rows(4 * n + s), 4 * n + s, :])
                                        for s in range(4 if n < 2 else 1)])
            pe.wait_ge(pg_landed, 16 * 32)
            for n in range(4):
                transposes(("ps", n), [(P * s, kpg[:, 4 * n + s, :]) for s in range(4)])
            for n in range(3):
                wait_evac(pe, "kiT", n)
                wait_evac(pe, "qi", 0, n)
                wait_evac(pe, "qi", 1, n)
            for b, h, c0, w_ in SCC:
                ps = begin("sc", b, h, c0, w_)
                q0 = 64 * (h % 2)
                done(pe.matmul(ps[:, 0:w_], qiT[q0:q0 + 64, h // 2, b * P:(b + 1) * P],
                               kiT[q0:q0 + 64, c0:c0 + w_], start=True, stop=True), "sc", b, h, c0, w_)
            pe.wait_ge(qis_done, 1)
            for n in range(4):
                wait_evac(pe, "ps", n)
            for g in range(2):
                ps = begin("wr", g)
                done(pe.matmul(ps[:, 0:IH], k32["exp_i"][:, g * P:(g + 1) * P], kw[0:NS, NTP, 64:68],
                               start=True, stop=True), "wr", g)
                ps = begin("si", g)
                for j in range(4):
                    b = 4 * g + j
                    for c0, cn, rhs in ((0, PAST, lambda: kiS[:, b, :]),
                                        (PAST, DT, lambda: kiT[:, SEQ + b * DT:SEQ + (b + 1) * DT])):
                        for hp in range(2):
                            ins = pe.matmul(ps[32 * j:32 * j + 32, c0:c0 + cn], qiS[:, 2 * b + hp, :], rhs(),
                                            start=hp == 0, stop=hp == 1)
                done(ins, "si", g)
            ps = begin("ss")
            for g in range(2):
                pe.wait_ge(rsw_done, g + 1)
                ins = pe.matmul(ps[0:NS, 0:NKS], k128["sum_i"][:, g * NS:(g + 1) * NS],
                                (rs_s, rl[0][:, 0:NKS])[g], start=g == 0, stop=g == 1)
            done(ins, "ss")

            for name in ("qd", "kd"):
                wait_w(pe, name)
                for f in range(4):
                    for n in range(3):
                        feature_major((name, f, n), wview(name), f * P, P, n)
            for f in range(4):
                for n in range(3):
                    wait_evac(pe, "kd", f, n)
            for i in range(NT):
                ps = begin("kt", i)
                for f in range(4):
                    ins = pe.transpose(ps[0:rows(i), f * P:(f + 1) * P], kdT[:, f, i * P:i * P + rows(i)], ident)
                done(ins, "kt", i)
            wait_w(pe, "vd")
            for i in range(NT):
                token_major(("vd", i), wview("vd"), 0, 512, i)

            def qk(u):
                b, h = UN[u]
                if u >= 2:
                    pe.wait_ge(lg_used, u - 1)
                p0 = 64 * (h % 2)
                L = P * (b + 1)
                for c0 in range(0, L, 512):
                    c1 = min(L, c0 + 512)
                    ins = pe.matmul(lgt[u % 2][:, c0:c1], qdT[p0:p0 + 64, h // 2, b * P:(b + 1) * P],
                                    kdT[p0:p0 + 64, h // 2, c0:c1], start=True, stop=True)
                ins.then_inc(lg_full, 1)

            def pv(u):
                b, h = UN[u]
                for c in range((b + 4) // 4):
                    wait_evac(pe, "pt", u, c)
                ps = begin("o", u)
                for s in range(b + 1):
                    ins = pe.matmul(ps[:, 0:DHD], pT[u % 2][:, s, :], vd[:, s, h * DHD:(h + 1) * DHD],
                                    start=s == 0, stop=s == b)
                done(ins, "o", u)
                if h == DH - 1:
                    wait_evac(pe, "o", u)
                    wait_evac(pe, "o", u - 1)
                    wait_evac(pe, "o", u - 2)
                    wait_evac(pe, "o", u - 3)
                    transposes(("ot", b), [(P * f, osb[b % 2][:, f * P:(f + 1) * P]) for f in range(4)])

            for n in range(3):
                for f in range(4):
                    wait_evac(pe, "qd", f, n)
            for i in range(NT):
                wait_evac(pe, "vd", i)
            qk(0)
            for u in range(len(UN) + 1):
                if u + 1 < len(UN):
                    qk(u + 1)
                if u >= 1:
                    pv(u - 1)
                if u < len(UN):
                    b = UN[u][0]
                    pe.wait_ge(pr_done, u + 1)
                    for c in range((b + 4) // 4):
                        transposes(("pt", u, c), [(P * (s - 4 * c), pr[u % 2][:, s * P:(s + 1) * P])
                                                  for s in range(4 * c, min(b + 1, 4 * c + 4))])

            def queries_keys(h):
                for f, key in enumerate(("gq", "gk")):
                    for n in range(3):
                        by_piece((key, h, n), 6 * h + f, n)

            pe.wait_ge(qbs_done, 1)
            pe.wait_ge(relt_done, 1)
            for g in range(2):
                for j in range(4):
                    b = 4 * g + j
                    pe.wait_ge(ks_landed[b % 2], 32 * (b // 2 + 1))
                    for p in range(NPG):
                        ps = begin("kp", g, j, p)
                        for f in range(4):
                            ins = pe.transpose(ps[:, f * P:(f + 1) * P], kpS[b % 2][:, p, f * P:(f + 1) * P], ident)
                        done(ins, "kp", g, j, p)
                    for p in range(NPG):
                        wait_evac(pe, "kp", g, j, p)
                    if j == 0:
                        pe.wait_ge(lg_used, len(UN))
                    for c0, cn in ((0, PAST), (PAST, DT)):
                        for f in range(4):
                            rhs = kTs[b % 2][:, f, :] if cn == PAST else kdT[:, f, SEQ + b * DT:SEQ + (b + 1) * DT]
                            ins = pe.matmul(lgt[g][32 * j:32 * j + 32, c0:c0 + cn], qbS[:, 4 * b + f, :], rhs,
                                            start=f == 0, stop=f == 3)
                    ins.then_inc(so_used, 1)
                ps = begin("mb", g)
                pe.matmul(ps[:, 0:NKS], k32["exp_h"][:, g * P:(g + 1) * P], scs[0:NS, :], start=True, stop=False)
                for t in range(DT):
                    ins = pe.matmul(ps[:, 0:NKS], relt[0:NB, t, :], k32["onehot"][:, 3 - t:3 - t + NKS],
                                    start=False, stop=t == DT - 1)
                done(ins, "mb", g)
            pe.wait_ge(n_lo_done, KD)
            queries_keys(0)
            for g in range(2):
                pe.wait_ge(spn, g + 1)
                ps = begin("sl", g)
                done(pe.transpose(ps[0:NS, 0:P], pnS.rearrange("p a b -> p (a b)"), ident), "sl", g)
                transposes(("spt", g), [(P * p, prS[g][:, p * P:(p + 1) * P]) for p in range(NPG)])
                wait_evac(pe, "sl", g)
                wait_evac(pe, "spt", g)
                pe.wait_ge(vs_landed[g], 16 * 4 * NPG)
                ps = begin("so", g)
                for j in range(4):
                    for p in range(NPG):
                        pe.matmul(ps[32 * j:32 * j + 32, :], ptS[:, p, 32 * j:32 * j + 32], vpS[4 * g + j][:, p, :],
                                  start=p == 0, stop=False)
                    ins = pe.matmul(ps[32 * j:32 * j + 32, :], ptS[0:NS, 2, 32 * j:32 * j + 32], vd[0:NS, NTP, :],
                                    start=False, stop=True)
                done(ins, "so", g)
                wait_evac(pe, "so", g)
                ps = begin("sot", g)
                for f in range(4):
                    ins = pe.matmul(ps[:, 16 * f:16 * f + 16], omS[:, f * P:(f + 1) * P], k128["sum_t"],
                                    start=True, stop=True)
                done(ins, "sot", g)

            def turn_outputs(h):
                for i in range(NT):
                    pe.wait_ge(on_done, NT * h + i + 1)
                    transposes(("gt", h, i), [(P * f, (vh[:, i, :] if i < NTP else o8[0:NS, :])[:, f * P:(f + 1) * P])
                                              for f in range(2)])

            def pair_products(h, i):
                t0 = i * P
                ps = begin("at", h, i)
                if i == NTP:
                    ins = pe.matmul(ps[0:NS, 0:NS], K1[:, t0:T], Q3[:, t0:T], start=True, stop=True)
                else:
                    pe.matmul(ps[0:64, 0:64], K1[:, t0:t0 + 64], Q1[:, t0:t0 + 64], start=True, stop=True)
                    pe.matmul(ps[0:64, 64:P], QK2[:, t0:t0 + 64], QK2[:, t0 + 64:t0 + P], start=True, stop=True)
                    ins = pe.matmul(ps[64:P, 64:P], K1[:, t0 + 64:t0 + P], Q1[:, t0 + 64:t0 + P],
                                    start=True, stop=True)
                done(ins, "at", h, i)
                ps = begin("k4", h, i)
                done(pe.transpose(ps[0:rows(i), 0:P], K4[:, t0:t0 + rows(i)], ident), "k4", h, i)

            for h in range(GH):
                if h >= 1:
                    queries_keys(h)
                if h >= 1:
                    turn_outputs(h - 1)
                pe.wait_ge(wgu_in, 16)
                for n in range(3):
                    ps = begin("gz", h, n)
                    done(pe.matmul(ps[:, 0:W3], wgu[0:RANK, h * GDK:(h + 1) * GDK],
                                   alT[0:RANK, n * W3:(n + 1) * W3], start=True, stop=True), "gz", h, n)
                pe.wait_ge(p_lo_done, 6 * h + 4)
                s_ = (6 * h + 2) % 4
                pair = [w_.rearrange("p (s k) n -> p s k n", k=KD)[:, s_:s_ + 2] for w_ in (pw_hi, pw_lo)]
                for i in range(NT):
                    ps = begin("gv", h, i)
                    out = ps[0:rows(i), 0:GDV].rearrange("p (s n) -> p s n", s=2)
                    t0, t1 = i * P, i * P + rows(i)
                    for kk in range(KD):
                        ins = three_passes(out, n_hi[kk][:, t0:t1], n_lo[kk][:, t0:t1], pair[0][:, :, kk, :],
                                           pair[1][:, :, kk, :], kk == 0, kk == KD - 1)
                    done(ins, "gv", h, i)
                for f in range(2):
                    for n in range(3):
                        by_piece(("gr", h, f, n), 6 * h + 4 + f, n)
                pe.wait_ge(f_done, 5 * (h + 1))
                for i in range(NT):
                    wait_evac(pe, "gv", h, i)
                pair_products(h, 0)
                for i in range(NTP):
                    pair_products(h, i + 1)
                    ps = begin("go", h, i)
                    wait_evac(pe, "at", h, i)
                    ins = pe.matmul(ps[:, 0:GDV], atb[i % 2], vh[:, i, :], start=True, stop=i == 0)
                    if i >= 1:
                        wait_evac(pe, "ds", h, i - 1)
                        ins = pe.matmul(ps[:, 0:GDV], Q3[:, i * P:(i + 1) * P], Sp, start=False, stop=True)
                    done(ins, "go", h, i)
                    wait_evac(pe, "k4", h, i)
                    ps = begin("ds", h, i)
                    done(pe.matmul(ps[:, 0:GDV], k4T[i % 2], vh[:, i, :], start=True, stop=True), "ds", h, i)
                ps = begin("go", h, NTP)
                wait_evac(pe, "at", h, NTP)
                pe.wait_ge(q3p_done, h + 1)
                pe.wait_ge(st_in, 16 * (h + 1))
                pe.matmul(ps[0:NS, 0:GDV], atS[0:NS, :], vh[0:NS, NTP, :], start=True, stop=False)
                for b in range(DB):
                    ins = pe.matmul(ps[0:NS, 0:GDV], q3p[:, b, :], S0[:, b, :], start=False, stop=b == DB - 1)
                done(ins, "go", h, NTP)
                pe.wait_ge(k4p_done, h + 1)
                for b in range(DB):
                    ps = begin("ds", h, NTP + b)
                    done(pe.matmul(ps[:, 0:GDV], k4p[0:NS, b, :], vh[0:NS, NTP, :], start=True, stop=True),
                         "ds", h, NTP + b)
            by_piece(("me", 0, 0), M0, 0)
            turn_outputs(GH - 1)
            tiles = lambda t_: [t_[:, k, :] for k in range(t_.shape[1])]
            for q, (gate, branch, f) in enumerate(ROUNDS_M):
                hi, lo, split = (od_hi, od_lo, od_lo_done) if branch == "mz" else (og_hi, og_lo, og_lo_done)
                for n in range(3):
                    if q or n:
                        by_piece((gate, f, n), M0 + 2 * q, n)
                for n in range(3):
                    by_piece((branch, f, n), M0 + 2 * q + 1, n, tiles(hi), tiles(lo), split if f == 0 and n == 0 else None)
            pe.wait_ge(z_done, 6 * KD)
            wait_w(pe, ("wo", 0))
            wait_w(pe, ("wo", 1))

            def h2_tile(i):
                pe.wait_ge(y_h, i + 1)
                for c in range(2):
                    transposes(("h2", i, c), [(P * s, h2[i % 2][0:rows(i), (4 * c + s) * P:(4 * c + s + 1) * P])
                                              for s in range(4)])
            for i in range(NT):
                for s in range(2):
                    token_major(("wo", i, s), wview(("wo", s)), 0, 512, i, src=zT)
                if i >= 2:
                    h2_tile(i - 2)
            h2_tile(NT - 2)
            h2_tile(NT - 1)
            def begin_ff(i, *key):
                pe.wait_ge(evac[chunk[key] % 4], i * PAIR + chunk[key] // 4)
                return bank(*key)

            def ff_unit(i, half, first=False):
                for f in range(2):
                    for n in range(3):
                        t0, tn = TCH[n]
                        if first and f == 0:
                            tiles = min(NT, -(-(t0 + tn) // P))
                            pe.wait_ge(h_lo_done, 2 * tiles)
                        for k, key in enumerate(("fg", "fu")):
                            if f == 0 and n == 0:
                                pe.wait_ge(w_lo_done[k], i * 2 + (half + 1))
                            ps = begin_ff(i, key, half, f, n)
                            for kk in range(KD):
                                ins = three_passes(ps[:, 0:tn], w_hi[k][:, kk, f * P:(f + 1) * P],
                                                   w_lo[k][:, kk, f * P:(f + 1) * P], h_hi[:, kk, t0:t0 + tn],
                                                   h_lo[:, kk, t0:t0 + tn], kk == 0, kk == KD - 1)
                            done(ins, key, half, f, n)
                pe.wait_ge(w_lo_done[2], i * 2 + (half + 1))
                waited = 0
                for j in range(NT):
                    t0, tn = j * P, rows(j)
                    need = 3 + -(-(t0 + tn) // W3)
                    if need > waited:
                        pe.wait_ge(a_lo_done, i * 12 + (6 * half + need))
                        waited = need
                    for c in range(2):
                        ps = begin_ff(i, "dn", half, j, c)
                        for kk in range(2):
                            ins = three_passes(ps[0:tn, :], a_hi[:, kk, t0:t0 + tn], a_lo[:, kk, t0:t0 + tn],
                                               w_hi[2][:, kk, 512 * c:512 * c + 512],
                                               w_lo[2][:, kk, 512 * c:512 * c + 512], kk == 0, kk == 1)
                        done(ins, "dn", half, j, c)

            ff_unit(0, 0, True)
            ff_unit(0, 1)
            with pe.Fori(1, PAIRS) as i:
                ff_unit(i, 0)
                ff_unit(i, 1)
            ff_unit(PAIRS, 0)

        @block.scalar
        def _(act):
            seq = [0]

            def link(ins):
                seq[0] += 1
                ins.then_inc(act_seq, 1)
                act.wait_ge(act_seq, seq[0])

            def copy_out(dst, src, *key, scale=1.0):
                wait_full(act, *key)
                evacuates(act.activation(dst, src, ACT.Copy, scale=scale), *key)

            act.wait_ge(c_landed, 16 * N_CONST)
            copy_out(vec, bank("vec")[:, 0:22], "vec")
            for i in range(NT + 1):
                if i < NT:
                    r = rows(i)
                    act.wait_ge(x_landed[i % 4], 16 * (i // 4 + 1))
                    if i >= 1:
                        act.wait_ge(x_sq, i)
                    act.activation(sqj[0:r, :], xa[i % 4][0:r, :], ACT.Square,
                                   accum_out=ssq[0:r, i:i + 1]).then_inc(x_sq, 1)
                if i >= 1:
                    r = rows(i - 1)
                    act.wait_ge(x_ms, i)
                    act.activation(rt[0:r, i - 1:i], msq[0:r, i - 1:i], ACT.Sqrt).then_inc(x_rt, 1)
            for f in range(2):
                for n in range(3):
                    copy_out(qiT[:, f, n * W3:(n + 1) * W3], bank("qi", f, n)[:, 0:W3], "qi", f, n)
            act.wait_ge(zeroed, 1)
            for i in range(NT):
                copy_out(kw[0:rows(i), i, :], bank("ki", i)[0:rows(i), 0:68], "ki", i)
            for n in range(3):
                copy_out(alT[0:RANK, n * W3:(n + 1) * W3], bank("al", n)[0:RANK, 0:W3], "al", n)
            act.wait_ge(kv_done, 1)
            act.activation(krt, kvar, ACT.Sqrt).then_inc(krt_done, 1)
            for n in range(3):
                w_ = 512 if n < 2 else NS
                copy_out(kiT[:, n * 512:n * 512 + w_], bank("kiT", n)[:, 0:w_], "kiT", n)
            for n in range(4):
                copy_out(kiS[:, 2 * n:2 * n + 2, :], bank("ps", n).rearrange("p (a b) -> p a b", a=2), "ps", n)
            for n, key in enumerate(SCC):
                if n >= 2:
                    act.wait_ge(rl_used, n - 1)
                wait_full(act, "sc", *key)
                w_ = key[3]
                evacuates(act.activation(rl[n % 2][:, 0:w_], bank("sc", *key)[:, 0:w_], ACT.Relu, scale=0.0625),
                          "sc", *key)
            for g in range(2):
                wait_full(act, "si", g)
                if g == 1:
                    act.wait_ge(rl_used, len(SCC))
                evacuates(act.activation((rs_s, rl[0][:, 0:NKS])[g], bank("si", g)[:, 0:NKS], ACT.Relu,
                                         scale=0.0625), "si", g)
            act.wait_ge(x_h, NT)
            for name, dst, sc in (("qd", qdT, 0.125), ("kd", kdT, 1.0)):
                for f in range(4):
                    for n in range(3):
                        if name == "qd" and f == 0 and n == 0:
                            wait_evac(act, "h", NT - 1, 0)
                            wait_evac(act, "h", NT - 1, 1)
                        copy_out(dst[:, f, n * W3:(n + 1) * W3], bank(name, f, n)[:, 0:W3], name, f, n, scale=sc)
            for i in range(NT):
                if i >= 2:
                    act.wait_ge(kt_out[i % 2], 16 * (i // 2))
                copy_out(kst[i % 2][0:rows(i), :], bank("kt", i)[0:rows(i), :], "kt", i)
            all_nb_out(act)
            for i in range(NT):
                copy_out(vd[0:rows(i), i, :], bank("vd", i)[0:rows(i), :], "vd", i)
            all_kt_out(act)
            for u, (b, h) in enumerate(UN):
                L = P * (b + 1)
                act.wait_ge(mx_done, u + 1)
                if u >= 2:
                    for c in range((UN[u - 2][0] + 4) // 4):
                        wait_evac(act, "pt", u - 2, c)
                link(act.activation(pr[u % 2][:, 0:L], nlg[u % 2][:, 0:L], ACT.Exp, bias=nmx[:, u % 4:u % 4 + 1],
                                    scale=-1.0, accum_out=rsum[:, u % 4:u % 4 + 1]))
                act.sem_inc(pr_done, 1)
                if b >= 4:
                    if u >= 2:
                        wait_full(act, "o", u - 2)
                    k = b - 3
                    copy_out(pT[u % 2][:, 4:4 + k, :], bank("pt", u, 1)[:, 0:k * P].rearrange("p (a b) -> p a b", b=P),
                             "pt", u, 1)
                if b >= 4 and h % 4 == 3:
                    k = 2 * (b - 4) + h // 4
                    act.activation(n_hi[k], hT[:, k, :], ACT.Copy).then_inc(n_hi_done, 1)
                if h == 0 and b >= 1:
                    copy_out(odT[:, :, (b - 1) * P:b * P], bank("ot", b - 1).rearrange("p (a b) -> p a b", a=4),
                             "ot", b - 1)
            copy_out(odT[:, :, SEQ - P:SEQ], bank("ot", NTP - 1).rearrange("p (a b) -> p a b", a=4), "ot", NTP - 1)
            def sample_exp(g):
                act.wait_ge(smx, g + 1)
                act.activation(prS[g], nlS[g], ACT.Exp, bias=nmx[:, g:g + 1], scale=-1.0,
                               accum_out=rsum[:, g:g + 1]).then_inc(spr, 1)

            def hi_piece(n):
                act.wait_ge(p_landed[n % 2], 16 * (n // 2 + 1))
                if n >= 4:
                    wait_full(act, *pieces[n - 4][3])
                raw, hi, _ = piece(n)
                act.activation(hi, raw, ACT.Copy).then_inc(p_hi_done, 1)

            def queries_keys(h):
                for key, dst in (("gq", qh), ("gk", kh)):
                    for n in range(3):
                        copy_out(dst[:, n * W3:(n + 1) * W3], bank(key, h, n)[:, 0:W3], key, h, n)

            for g in range(2):
                for j in range(4):
                    b = 4 * g + j
                    if b >= 2:
                        act.wait_ge(so_used, b - 1)
                    for p in range(NPG):
                        copy_out(kTs[b % 2][:, :, p * P:(p + 1) * P],
                                 bank("kp", g, j, p).rearrange("p (a b) -> p a b", a=4), "kp", g, j, p)
                copy_out(mbS[g], bank("mb", g)[:, 0:NKS], "mb", g)
                if g == 0:
                    hi_piece(0)
                    hi_piece(1)
                else:
                    sample_exp(0)
            sample_exp(1)

            queries_keys(0)
            for g in range(2):
                if g == 1:
                    wait_full(act, "so", 0)
                copy_out(ptS[0:NS, 2, :], bank("sl", g)[0:NS, 0:P], "sl", g)
                copy_out(ptS[:, 0:2, :], bank("spt", g)[:, 0:2 * P].rearrange("p (a b) -> p a b", b=P), "spt", g)
                copy_out(odT[:, :, SEQ + 16 * g:SEQ + 16 * g + 16],
                         bank("sot", g)[:, 0:64].rearrange("p (a b) -> p a b", a=4), "sot", g)
                if g == 0:
                    hi_piece(2)
                    hi_piece(3)
            nsg = 0
            for h in range(GH):
                if h >= 1:
                    act.wait_ge(f_done, 5 * h)
                    queries_keys(h)
                for n in (6 * h + 4, 6 * h + 5):
                    hi_piece(n)
                for n in range(3):
                    wait_full(act, "gz", h, n)
                    ins = act.activation(uT[:, n * W3:(n + 1) * W3], bank("gz", h, n)[:, 0:W3], ACT.Identity,
                                         bias=vec[:, 16 + h:17 + h])
                    evacuates(ins, "gz", h, n)
                for n in range(3):
                    wait_evac(act, "gz", h, n)
                link(act.activation(eT, uT, ACT.Abs))
                link(act.activation(eT, eT, ACT.Exp, scale=-1.0))
                act.activation(eT, eT, ACT.Ln, bias=one).then_inc(sp_done, 1)
                if h >= 1:
                    wait_full(act, "gt", h - 1, NTP)
                for m in range(NT):
                    r = rows(m)
                    copy_out(vh[0:r, m, :], bank("gv", h, m)[0:r, 0:GDV], "gv", h, m)
                    if m >= 5:
                        continue
                    act.wait_ge(d_done, 5 * h + m + 1)
                    if m >= 1:
                        act.wait_ge(f_done, 5 * h + m)
                    if m == 2:
                        act.activation(eT[:, 0:SEQ].rearrange("p (c s) -> p c s", s=P)[:, :, 0:64],
                                       dT[:, 0:SEQ].rearrange("p (c s) -> p c s", s=P)[:, :, 0:64],
                                       ACT.Exp, scale=-1 / 16)
                        act.activation(eT[:, 0:SEQ].rearrange("p (c s) -> p c s", s=P)[:, :, 64:P],
                                       dT[:, 0:SEQ].rearrange("p (c s) -> p c s", s=P)[:, :, 64:P],
                                       ACT.Exp, scale=1 / 16).then_inc(e_done, 1)
                    else:
                        act.activation(eT, Bc if m == 3 else dT, ACT.Exp,
                                       scale=(1 / 16, -1 / 16, 0, 1 / 16, -1 / 16)[m]).then_inc(e_done, 1)
                for f in range(2):
                    for n in range(3):
                        wait_full(act, "gr", h, f, n)
                        if nsg >= 2:
                            k = nsg - 2
                            wait_evac(act, "gr", k // 6, k % 6 // 3, k % 3)
                        act.activation(sig[nsg % 2], bank("gr", h, f, n)[:, 0:W3], ACT.Sigmoid).then_inc(sg_done, 1)
                        nsg += 1
                        if h + 1 < GH and n >= 1:
                            hi_piece(6 * (h + 1) + 2 * f + n - 1)

                def turned_keys(i):
                    if 2 <= i < NTP:
                        wait_full(act, "ds", h, i - 2)
                    if i == NTP:
                        wait_full(act, "ds", h, NTP - 2)
                    copy_out(k4T[i % 2][0:rows(i), :], bank("k4", h, i)[0:rows(i), 0:P], "k4", h, i)

                turned_keys(0)
                for i in range(NTP):
                    turned_keys(i + 1)
                    wait_full(act, "ds", h, i)
                    copy_out(vh[:, i, :], bank("go", h, i)[:, 0:GDV], "go", h, i)
                copy_out(o8[0:NS, :], bank("go", h, NTP)[0:NS, 0:GDV], "go", h, NTP)
                if h == GH - 1:
                    act.wait_ge(f_done, 5 * GH)
                    wait_evac(act, "gr", h, 1, 2)
                    hi_piece(M0)
                    hi_piece(M0 + 1)
                for i in range(NT):
                    wait_evac(act, "go", h, i)
                    r = rows(i)
                    src = vh[:, i, :] if i < NTP else o8[0:r, :]
                    if i >= 1:
                        act.wait_ge(act_seq, seq[0])
                    seq[0] += 1
                    act.activation(gsq[0:r, :], src, ACT.Square, accum_out=oss[0:r, i:i + 1]).then_inc(act_seq, 1)
                act.wait_ge(act_seq, seq[0])
                act.sem_inc(oss_done, 1)
                act.wait_ge(oms_done, h + 1)
                act.activation(ort, oms, ACT.Sqrt).then_inc(ort_done, 1)
            m = 0
            for q, (gate, branch, f) in enumerate(ROUNDS_M):
                if q == KD:
                    act.wait_ge(og_landed, 16 * KD)
                    wait_full(act, "mz", KD - 1, 2)
                    for k in range(KD):
                        act.activation(og_hi[:, k, :], og_whole[:, k, :], ACT.Copy).then_inc(og_hi_done, 1)
                for n in range(3):
                    if n == 2:
                        if q == 0:
                            act.wait_ge(od_landed, 16)
                            act.wait_ge(st_out, 32 * GH)
                            for k in range(4):
                                act.activation(od_hi[:, k, :], od_whole[:, k, :], ACT.Copy).then_inc(od_hi_done, 1)
                        if q + 1 < 2 * KD:
                            hi_piece(M0 + 2 * q + 2)
                            hi_piece(M0 + 2 * q + 3)
                    if m >= 2:
                        act.wait_ge(z_done, m - 1)
                    if m == 0:
                        act.wait_ge(core_done, 2 * GH)
                    if m == 1:
                        for i in range(NT):
                            wait_evac(act, "gt", GH - 1, i)
                    wait_full(act, gate, f, n)
                    evacuates(act.activation(msg[m % 2], bank(gate, f, n)[:, 0:W3], ACT.Sigmoid), gate, f, n)
                    m += 1
            def hi_tile(i):
                r = rows(i)
                for c in range(2):
                    wait_evac(act, "h2", i, c)
                    act.activation(h_hi[:, 4 * c:4 * c + 4, i * P:i * P + r], h2t[c][:, :, 0:r],
                                   ACT.Copy).then_inc(h_hi_done, 1)

            for i in range(NT):
                r = rows(i)
                act.wait_ge(r_used, 2 * (i + 1))
                if i >= 1:
                    act.wait_ge(act_seq, seq[0])
                link(act.activation(sq_out[0:r, :], x2[0:r, i, :], ACT.Square, accum_out=ssq[0:r, i:i + 1]))
                act.sem_inc(y_sq, 1)
                if i >= 2:
                    hi_tile(i - 2)
                act.wait_ge(y_ms, i + 1)
                act.activation(rt[0:r, i:i + 1], msq[0:r, i:i + 1], ACT.Sqrt).then_inc(y_rt, 1)
            def split(k, i, u1):
                act.wait_ge(raw_landed[k], i * 32 + 16 * u1)
                act.activation(w_hi[k], wraw[k], ACT.Copy).then_inc(w_hi_done[k], 1)

            wait_full(act, "wo", NT - 1, 0)
            wait_full(act, "wo", NT - 1, 1)
            for k in range(2):
                split(k, 0, 1)
                hi_tile(NT - 2 + k)
            def ff_unit(i, half, last=False):
                before = ("dn", 1 - half, NT - 1, 1)
                wait_full(act, *before, more=i * PAIR + (PAIR * (half - 1)))
                split(2, i, half + 1)
                for m in range(6):
                    f, n = m // 3, m % 3
                    wait_full(act, "fg", half, f, n, more=i * PAIR)
                    if m >= 2:
                        wait_evac(act, "fg", half, (m - 2) // 3, (m - 2) % 3, more=i * PAIR)
                    act.activation(fsig[m % 2], bank("fg", half, f, n)[:, 0:W3], ACT.Sigmoid).then_inc(f_sig, 1)
                    wait_evac(act, "fu", half, f, n, more=i * PAIR)
                    act.activation(a_hi[:, f, n * W3:(n + 1) * W3], ft, ACT.Copy).then_inc(a_hi_done, 1)
                if not last:
                    wait_full(act, "fg", half, 1, 2, more=i * PAIR)
                    split(0, i, half + 2)
                    wait_full(act, "fu", half, 1, 2, more=i * PAIR)
                    split(1, i, half + 2)

            act.wait_ge(h_lo_done, 2 * NT)
            with act.Fori(0, PAIRS) as i:
                ff_unit(i, 0)
                ff_unit(i, 1)
            ff_unit(PAIRS, 0, True)
            for i in range(NT):
                r = rows(i)
                act.wait_ge(x2_done, i + 1)
                link(act.activation(sq_out[0:r, :], x2[0:r, i, :], ACT.Square, accum_out=ssq[0:r, i:i + 1]))
                act.sem_inc(z_sq, 1)
                act.wait_ge(z_ms, i + 1)
                act.activation(rt[0:r, i:i + 1], msq[0:r, i:i + 1], ACT.Sqrt).then_inc(z_rt, 1)

        @block.vector
        def _(v):
            seq = [0]

            def link(ins):
                seq[0] += 1
                ins.then_inc(dve_seq, 1)
                v.wait_ge(dve_seq, seq[0])

            def bc(col, shape, axis):
                return col.unsqueeze(axis).to_broadcast(shape)

            link(v.memset(one, 1.0))
            link(v.memset(cnt, 1.0))
            v.wait_ge(c_landed, 16 * N_CONST)
            for h in range(DH):
                v.tensor_copy(relx[0:NB, h, :], relb[0:NB, h:h + 1].to_broadcast([NB, P]))
            link(v.memset(oss, 1.0))
            v.sem_inc(relx_done, 1)
            wait_evac(v, "vec")

            def mean_tile(i, s_sq, s_ms):
                r = rows(i)
                v.wait_ge(s_sq, i + 1)
                v.tensor_scalar(msq[0:r, i:i + 1], ssq[0:r, i:i + 1], 1.0 / D, EPS, ALU.mult, ALU.add).then_inc(s_ms, 1)

            def norm_tile(i, src, dst, s_rt, s_h):
                r = rows(i)
                v.wait_ge(s_rt, i + 1)
                link(v.reciprocal(rstd[0:r, i:i + 1], rt[0:r, i:i + 1]))
                v.tensor_scalar(dst[0:r, :], src[0:r, :], rstd[0:r, i:i + 1], None, ALU.mult).then_inc(s_h, 1)

            def turn_tile(i, gains, key, out):
                r = rows(i)
                for c in range(2):
                    wait_full(v, key, i, c)
                    g = gains[:, 4 * c:4 * c + 4].unsqueeze(2).to_broadcast([P, 4, r])
                    src = bank(key, i, c).rearrange("p (a b) -> p a b", a=4)[:, :, 0:r]
                    evacuates(v.tensor_tensor(out[:, 4 * c:4 * c + 4, i * P:i * P + r], src, g, ALU.mult), key, i, c)

            for i in range(NT + 2):
                if i < NT:
                    mean_tile(i, x_sq, x_ms)
                if 1 <= i <= NT:
                    norm_tile(i - 1, xa[(i - 1) % 4], xa[(i - 1) % 4], x_rt, x_h)
                if i >= 2:
                    turn_tile(i - 2, vec[:, 0:8], "h", hT)
                    v.sem_inc(x_used, 1)
            for h in range(DH):
                wait_full(v, "nb", h)
                link(v.tensor_copy(r31[:, h:h + 1], bank("nb", h)[:, 0:1]))
                if h >= 2:
                    v.wait_ge(nb_out[h % 2], 16 * (h // 2))
                evacuates(v.tensor_scalar(nbs[h % 2], bank("nb", h)[:, 0:383], r31[:, h:h + 1], None, ALU.subtract),
                          "nb", h)
            for i in range(NT):
                wait_evac(v, "ki", i)
            kv = kw[:, :, 0:IDM]
            link(v.tensor_reduce(kmu, kv, X, ALU.add))
            link(v.tensor_scalar(kmu, kmu, 1.0 / IDM, None, ALU.mult))
            link(v.tensor_tensor(kd2, kv, bc(kmu, [P, NT, IDM], 2), ALU.subtract))
            link(v.tensor_tensor(kn[:, :, 0:IDM], kd2, kd2, ALU.mult))
            link(v.tensor_reduce(kvar, kn[:, :, 0:IDM], X, ALU.add))
            link(v.tensor_scalar(kvar, kvar, 1.0 / IDM, EPS, ALU.mult, ALU.add))
            v.sem_inc(kv_done, 1)
            v.wait_ge(krt_done, 1)
            link(v.reciprocal(krs, krt))
            link(v.tensor_tensor(kd2, kd2, bc(krs, [P, NT, IDM], 2), ALU.mult))
            link(v.tensor_tensor(kd2, kd2, bc(kg_b, [P, NT, IDM], 1), ALU.mult))
            link(v.tensor_tensor(kn[:, :, 0:IDM], kd2, bc(kb_b, [P, NT, IDM], 1), ALU.add))
            link(v.tensor_tensor(kn[:, :, IDM:P], kd2, bc(kb_b, [P, NT, IDM], 1), ALU.add))
            v.sem_inc(kn_done, 1)
            v.wait_ge(zeroed, 2)
            for n in range(3):
                wait_evac(v, "qi", 0, n)
                wait_evac(v, "qi", 1, n)
            q4 = qiS.rearrange("p (b f) (h t) -> p b f h t", f=2, t=DT)
            for f in range(2):
                for e in range(2):
                    src = qiT[64 * e:64 * e + 64, f, SEQ:T].rearrange("p (b t) -> p b t", t=DT)
                    ins = v.tensor_copy(q4[64 * e:64 * e + 64, :, f, 2 * f + e, :], src)
            link(ins)
            v.sem_inc(qis_done, 1)
            for n, (b, h, c0, w_) in enumerate(SCC):
                wait_evac(v, "sc", b, h, c0, w_)
                dst = SC[:, SCAT[b] + c0:SCAT[b] + c0 + w_]
                wt = kw[:, b, 64 + h:65 + h]
                if h == 0:
                    ins = v.tensor_scalar(dst, rl[n % 2][:, 0:w_], wt, None, ALU.mult)
                else:
                    ins = v.scalar_tensor_tensor(dst, rl[n % 2][:, 0:w_], wt, dst, ALU.mult, ALU.add)
                ins.then_inc(rl_used, 1)
                v.wait_ge(rl_used, n + 1)
                if h == IH - 1 and c0 + w_ == P * (b + 1):
                    v.sem_inc(sc_done, 1)
            for g in range(2):
                wait_full(v, "wr", g)
                link(v.tensor_tensor(wtmp, bank("wr", g)[:, 0:IH], k128["pick_i"], ALU.mult))
                evacuates(v.tensor_reduce(wrow[:, g:g + 1], wtmp, X, ALU.add), "wr", g)
                wait_evac(v, "wr", g)
                wait_evac(v, "si", g)
                buf = (rs_s, rl[0][:, 0:NKS])[g]
                v.tensor_scalar(buf, buf, wrow[:, g:g + 1], None, ALU.mult).then_inc(rsw_done, 1)
            v.wait_ge(zeroed, 3)
            wait_full(v, "ss")
            link(v.tensor_copy(scs[0:NS, 0:PAST], bank("ss")[0:NS, 0:PAST]))
            evacuates(v.tensor_tensor(scs[0:NS, PAST:NKS], bank("ss")[0:NS, PAST:NKS], k32["future"], ALU.add), "ss")
            wait_evac(v, "ss")

            v.wait_ge(sc_diag, NTP - 2)
            spans = [(SCAT[b], P * (b + 1), 0.0) for b in range(2, NTP)] + [(_n, NKS, float(TOPK - TOPK_S))]
            GRP = [(0, 4), (4, 7)]
            link(v.memset(cand, 0))

            def count(k):
                s0, n_, init = spans[k]
                return v.tensor_scalar(junk[:, s0:s0 + n_], SC[:, s0:s0 + n_], cand[:, k:k + 1].bitcast(F32), init,
                                       ALU.is_ge, ALU.add, accum_out=cnt[:, k:k + 1])

            def try_bit(g, b):
                lo, hi = GRP[g]
                return v.tensor_scalar(cand[:, lo:hi], thr[:, lo:hi], bits[:, b], None, ALU.bitwise_xor)

            def keep(g, b):
                lo, hi = GRP[g]
                return v.tensor_scalar(gbit[:, lo:hi], cnt[:, lo:hi], float(TOPK), k128["bits_f"][:, b],
                                       ALU.is_ge, ALU.mult)

            def set_bit(g):
                lo, hi = GRP[g]
                return v.tensor_tensor(thr[:, lo:hi], thr[:, lo:hi], gbit[:, lo:hi], ALU.bitwise_xor)

            for k in range(7):
                ins = count(k)
            link(ins)
            link(v.tensor_scalar(thr, cnt, float(TOPK), 1.0, ALU.is_ge, ALU.subtract))
            link(try_bit(0, slice(0, 1)))
            link(try_bit(1, slice(0, 1)))
            for k in range(4):
                ins = count(k)
            link(ins)
            step0 = seq[0]
            PER = 10
            ROUNDS = 30

            with v.Fori(0, ROUNDS) as r:
                at_step = lambda n: v.wait_ge(dve_seq, r * PER + (step0 + n))
                inc_ = lambda ins: ins.then_inc(dve_seq, 1)
                inc_(count(4))
                at_step(0)
                inc_(keep(0, bass.ds(r, 1)))
                inc_(count(5))
                at_step(2)
                inc_(set_bit(0))
                inc_(count(6))
                at_step(4)
                inc_(try_bit(0, bass.ds(r + 1, 1)))
                at_step(6)
                count(0)
                count(1)
                inc_(keep(1, bass.ds(r, 1)))
                count(2)
                at_step(7)
                inc_(set_bit(1))
                at_step(8)
                inc_(try_bit(1, bass.ds(r + 1, 1)))
                inc_(count(3))
                at_step(9)
            seq[0] = step0 + ROUNDS * PER
            v.wait_ge(dve_seq, seq[0])
            for k in range(4, 7):
                ins = count(k)
            link(ins)
            for g in range(2):
                link(keep(g, slice(ROUNDS, ROUNDS + 1)))
                link(set_bit(g))

            def mask_step(k, n):
                s0, n_, init = spans[k]
                s_, t_ = SC[:, s0:s0 + n_], thr[:, k:k + 1].bitcast(F32)
                if n == 0:
                    link(v.tensor_scalar(inc[:, 0:n_], s_, t_, init, ALU.is_gt, ALU.add, accum_out=cnt[:, k:k + 1]))
                elif n == 1:
                    link(v.tensor_scalar(need[:, k:k + 1], cnt[:, k:k + 1], -1.0, float(TOPK), ALU.mult, ALU.add))
                    link(v.tensor_scalar(eqc[:, 0:n_], s_, t_, None, ALU.is_equal))
                elif n == 2:
                    link(v.tensor_tensor_scan(inc[:, 0:n_], eqc[:, 0:n_], eqc[:, 0:n_], 0.0, ALU.add, ALU.max))
                elif n == 3:
                    link(v.scalar_tensor_tensor(eqc[:, 0:n_], inc[:, 0:n_], need[:, k:k + 1], eqc[:, 0:n_],
                                                ALU.is_le, ALU.mult))
                elif n == 4:
                    link(v.scalar_tensor_tensor(inc[:, 0:n_], s_, t_, eqc[:, 0:n_], ALU.is_gt, ALU.max))
                elif n == 5:
                    link(v.tensor_scalar(s_, inc[:, 0:n_], 1.0, -NEG, ALU.subtract, ALU.mult))
                    v.sem_inc(mask_done, 1)

            v.wait_ge(nb_in, 16 * DH)
            wait_evac(v, "vd", NTP)
            all_kt_out(v)
            v.wait_ge(ki_out, 32)

            def norm_head(u):
                b, h = UN[u]
                wait_full(v, "o", u)
                link(v.reciprocal(rrec[:, u % 4:u % 4 + 1], rsum[:, u % 4:u % 4 + 1]))
                if h == 0 and b >= 2:
                    wait_full(v, "ot", b - 2)
                evacuates(v.tensor_scalar(osb[b % 2][:, h * DHD:(h + 1) * DHD], bank("o", u)[:, 0:DHD],
                                          rrec[:, u % 4:u % 4 + 1], None, ALU.mult), "o", u)

            def logits(u):
                b, h = UN[u]
                L = P * (b + 1)
                near = min(L, 256)
                v.wait_ge(lg_full, u + 1)
                v.wait_ge(near_done, u + 1)
                if u >= 2:
                    v.wait_ge(pr_done, u - 1)
                c = u % 4
                if L > near:
                    link(v.tensor_tensor_reduce(nlg[u % 2][:, 0:L - near], lgt[u % 2][:, 0:L - near],
                                                SC[:, SCAT[b]:SCAT[b] + L - near], -1.0, 3e38, ALU.add, ALU.min,
                                                mxa[:, c:c + 1]))
                ini = mxa[:, c:c + 1] if L > near else 3e38
                link(v.tensor_tensor_reduce(nlg[u % 2][:, L - near:L], lgt[u % 2][:, L - near:L],
                                            nearm[c][:, 256 - near:256], -1.0, ini, ALU.add, ALU.min,
                                            nmx[:, c:c + 1]))
                v.sem_inc(mx_done, 1)
                v.sem_inc(lg_used, 1)

            logits(0)
            for u, (b, h) in enumerate(UN):
                if u + 1 < len(UN):
                    logits(u + 1)
                if u >= 1:
                    norm_head(u - 1)
                if b >= 1 and 1 <= h <= 6:
                    mask_step(b - 1, h - 1)
                k = min(b + 1, 4)
                wait_full(v, "pt", u, 0)
                if u >= 2:
                    wait_full(v, "o", u - 2)
                evacuates(v.tensor_copy(pT[u % 2][:, 0:k, :], bank("pt", u, 0)[:, 0:k * P].rearrange(
                    "p (a b) -> p a b", b=P)), "pt", u, 0)
                if b >= 4 and h % 4 == 3:
                    k = 2 * (b - 4) + h // 4
                    v.wait_ge(n_hi_done, k + 1)
                    v.tensor_tensor(n_lo[k], hT[:, k, :], n_hi[k], ALU.subtract)\
                     .then_inc(n_lo_done, 1)
            norm_head(len(UN) - 1)

            wait_full(v, "ot", NTP - 1)
            link(v.memset(qbS, 0.0))
            link(v.memset(relt[0:NB], 0.0))
            q5 = qbS.rearrange("p (b f) (h t) -> p b f h t", f=4, t=DT)
            for f in range(4):
                for e in range(2):
                    src = qdT[64 * e:64 * e + 64, f, SEQ:T].rearrange("p (b t) -> p b t", t=DT)
                    ins = v.tensor_copy(q5[64 * e:64 * e + 64, :, f, 2 * f + e, :], src)
            link(ins)
            v.sem_inc(qbs_done, 1)
            r4 = relt.rearrange("p t (j h u) -> p t j h u", j=4, u=DT)
            for t in range(DT):
                for j in range(4):
                    ins = v.tensor_copy(r4[0:NB, t, j, :, t], relb[0:NB, :])
            link(ins)
            v.sem_inc(relt_done, 1)
            def lo_piece(n):
                v.wait_ge(p_hi_done, n + 1)
                raw, hi, lo = piece(n)
                v.tensor_tensor(lo, raw, hi, ALU.subtract).then_inc(p_lo_done, 1)

            for g in range(2):
                v.wait_ge(so_used, 4 * (g + 1))
                wait_evac(v, "mb", g)
                v.tensor_tensor_reduce(nlS[g], lgt[g][:, 0:NKS], mbS[g], -1.0, 3e38, ALU.add, ALU.min,
                                       nmx[:, g:g + 1]).then_inc(smx, 1)
                if g == 0:
                    lo_piece(0)
                    lo_piece(1)
            for g in range(2):
                v.wait_ge(spr, g + 1)
                if g == 1:
                    wait_full(v, "sl", 0)
                pb_ = k128["pick_b"][:, g * DB:(g + 1) * DB].unsqueeze(2).to_broadcast([P, DB, DT])
                v.tensor_tensor(pnS, prS[g][:, PAST:NKS].unsqueeze(1).to_broadcast([P, DB, DT]), pb_,
                                ALU.mult).then_inc(spn, 1)
                link(v.reciprocal(rrec[:, g:g + 1], rsum[:, g:g + 1]))
                wait_full(v, "so", g)
                if g == 1:
                    wait_full(v, "sot", 0)
                evacuates(v.scalar_tensor_tensor(
                    omS.rearrange("p (h d) -> p h d", h=DH), bank("so", g).rearrange("p (h d) -> p h d", h=DH),
                    rrec[:, g:g + 1], k128["pick_h"].unsqueeze(2).to_broadcast([P, DH, DHD]),
                    ALU.mult, ALU.mult), "so", g)
                if g == 0:
                    lo_piece(2)
                    lo_piece(3)

            ngr = 0
            c64 = lambda t_: t_[:, 0:SEQ].rearrange("p (c s) -> p c s", s=64)
            c128_ = lambda t_: t_[:, 0:SEQ].rearrange("p (c s) -> p c s", s=P)
            c4 = lambda t_: t_[:, SEQ:T].rearrange("p (c s) -> p c s", s=DT)
            QS = float(GDK) ** -0.5
            for h in range(GH):
                for n in (6 * h + 4, 6 * h + 5):
                    lo_piece(n)
                if h == 0:
                    v.wait_ge(sp_done, 1)
                    for b_ in atb:
                        link(v.memset(b_, 0.0))
                    v.wait_ge(zeroed, 4)
                    v.wait_ge(od_out, 16)
                for n in range(3):
                    wait_evac(v, "gq", h, n)
                    wait_evac(v, "gk", h, n)
                    wait_evac(v, "gz", h, n)
                v.wait_ge(sp_done, h + 1)
                link(v.scalar_tensor_tensor(uT, uT, 0.0, eT, ALU.min, ALU.subtract))
                link(v.tensor_tensor_scan(Bc, rst, uT, 0.0, ALU.mult, ALU.add))
                if h >= 1:
                    wait_full(v, "gt", h - 1, NTP)
                mid = c64(Bc)[:, :, 31:32].to_broadcast([P, 16, 64])
                link(v.tensor_tensor(c64(dT), c64(Bc), mid, ALU.subtract))
                link(v.tensor_copy(dT[:, SEQ:T], Bc[:, SEQ:T]))
                v.sem_inc(d_done, 2)

                def product(m, dst, q, part=None):
                    v.wait_ge(e_done, 5 * h + m + 1)
                    pick = part or (lambda t_: t_)
                    if q:
                        ins = v.scalar_tensor_tensor(pick(dst), pick(qh), QS, pick(eT), ALU.mult, ALU.mult)
                    else:
                        ins = v.tensor_tensor(pick(dst), pick(kh), pick(eT), ALU.mult)
                    return ins

                link(product(0, Q1, True))
                v.sem_inc(f_done, 1)
                link(product(1, K1, False))
                link(v.tensor_tensor(c128_(dT), c128_(Bc), c128_(Bc)[:, :, 63:64].to_broadcast([P, 8, P]),
                                     ALU.subtract))
                v.sem_inc(d_done, 1)
                v.sem_inc(f_done, 1)
                link(product(2, QK2, False, lambda t_: c128_(t_)[:, :, 0:64]))
                link(product(2, QK2, True, lambda t_: c128_(t_)[:, :, 64:P]))
                link(v.tensor_tensor(c128_(dT), c128_(Bc), c128_(Bc)[:, :, P - 1:P].to_broadcast([P, 8, P]),
                                     ALU.subtract))
                link(v.tensor_tensor(c4(dT), c4(Bc), c4(Bc)[:, :, DT - 1:DT].to_broadcast([P, DB, DT]),
                                     ALU.subtract))
                v.sem_inc(d_done, 2)
                v.sem_inc(f_done, 1)
                link(product(3, Q3, True))
                link(v.tensor_copy(ebl[:, 0:NTP], c128_(eT)[:, :, P - 1]))
                link(v.tensor_copy(ebl[:, NTP:NTP + DB], c4(eT)[:, :, DT - 1]))
                v.sem_inc(f_done, 1)
                link(product(4, K4, False))
                v.sem_inc(f_done, 1)
                link(v.tensor_tensor(q3p, Q3[:, SEQ:T].unsqueeze(1).to_broadcast([P, DB, NS]),
                                     k128["cols_b"].rearrange("p (a b) -> p a b", a=DB), ALU.mult))
                v.sem_inc(q3p_done, 1)
                for f in range(2):
                    for n in range(3):
                        v.wait_ge(sg_done, ngr + 1)
                        evacuates(v.scalar_tensor_tensor(rh[:, f, n * W3:(n + 1) * W3], bank("gr", h, f, n)[:, 0:W3],
                                                         vec[:, 20 + f:21 + f], sig[ngr % 2], ALU.mult, ALU.mult),
                                  "gr", h, f, n)
                        ngr += 1
                        if h + 1 < GH and n >= 1:
                            lo_piece(6 * (h + 1) + 2 * f + n - 1)

                def mask_pairs(i):
                    wait_full(v, "at", h, i)
                    bk = bank("at", h, i)
                    if i == NTP:
                        evacuates(v.tensor_tensor(atS[0:NS, :], bk[0:NS, 0:NS], k32["same"], ALU.mult), "at", h, i)
                        return
                    if i >= 2:
                        wait_full(v, "go", h, i - 2)
                    v.tensor_tensor(atb[i % 2][0:64, :], bk[0:64, 0:P], k128["causal"][0:64, :], ALU.mult)
                    evacuates(v.tensor_tensor(atb[i % 2][64:P, 64:P], bk[64:P, 64:P], k128["causal"][64:P, 64:P],
                                              ALU.mult), "at", h, i)

                mask_pairs(0)
                for i in range(NTP):
                    mask_pairs(i + 1)
                    wait_full(v, "ds", h, i)
                    wait_full(v, "go", h, i)
                    if i == 0:
                        if h >= 1:
                            v.wait_ge(st_out, 16 * 2 * h)
                        ins = v.tensor_copy(Sp, bank("ds", h, i)[:, 0:GDV])
                    else:
                        ins = v.scalar_tensor_tensor(Sp, Sp, ebl[:, i:i + 1], bank("ds", h, i)[:, 0:GDV],
                                                     ALU.mult, ALU.add)
                    evacuates(ins, "ds", h, i)
                    wait_evac(v, "ds", h, i)
                v.sem_inc(core_done, 1)
                wait_evac(v, "k4", h, NTP)
                link(v.tensor_tensor(k4p[0:NS], k4T[0][0:NS, :].unsqueeze(1).to_broadcast([NS, DB, P]),
                                     k32["rows_b"].unsqueeze(2).to_broadcast([NS, DB, P]), ALU.mult))
                v.sem_inc(k4p_done, 1)
                wait_full(v, "go", h, NTP)
                for b in range(DB):
                    wait_full(v, "ds", h, NTP + b)
                    evacuates(v.scalar_tensor_tensor(S0[:, b, :], S0[:, b, :], ebl[:, NTP + b:NTP + b + 1],
                                                     bank("ds", h, NTP + b)[:, 0:GDV], ALU.mult, ALU.add),
                              "ds", h, NTP + b)
                for b in range(DB):
                    wait_evac(v, "ds", h, NTP + b)
                v.sem_inc(core_done, 1)
                if h == GH - 1:
                    lo_piece(M0)
                    lo_piece(M0 + 1)
                v.wait_ge(oss_done, h + 1)
                link(v.tensor_scalar(oms, oss, 1.0 / GDV, EPS, ALU.mult, ALU.add))
                v.sem_inc(oms_done, 1)
                v.wait_ge(ort_done, h + 1)
                link(v.reciprocal(ors, ort))
                if h >= 1:
                    v.wait_ge(og_out, 16 * h)
                for i in range(NT + 2):
                    if i < NT:
                        r = rows(i)
                        row = vh[:, i, :] if i < NTP else o8[0:r, :]
                        v.tensor_scalar(row, row, ors[0:r, i:i + 1], None, ALU.mult).then_inc(on_done, 1)
                    if i >= 2:
                        k = i - 2
                        r = rows(k)
                        wait_full(v, "gt", h, k)
                        src = bank("gt", h, k)[:, 0:2 * P].rearrange("p (a b) -> p a b", a=2)[:, :, 0:r]
                        evacuates(v.tensor_tensor(ogs[:, :, k * P:k * P + r], src,
                                                  rh[:, :, k * P:k * P + r], ALU.mult), "gt", h, k)

            for k in range(4):
                v.wait_ge(od_hi_done, k + 1)
                v.tensor_tensor(od_lo[:, k, :], od_whole[:, k, :], od_hi[:, k, :], ALU.subtract).then_inc(od_lo_done, 1)
            v.wait_ge(og_out, 16 * GH)
            m = 0
            for q, (gate, branch, f) in enumerate(ROUNDS_M):
                if q == KD:
                    for k in range(KD):
                        v.wait_ge(og_hi_done, k + 1)
                        v.tensor_tensor(og_lo[:, k, :], og_whole[:, k, :], og_hi[:, k, :], ALU.subtract)\
                         .then_inc(og_lo_done, 1)
                if q + 1 < 2 * KD:
                    lo_piece(M0 + 2 * q + 2)
                for n in range(3):
                    z = zT[:, f, n * W3:(n + 1) * W3]
                    wait_full(v, branch, f, n)
                    wait_evac(v, gate, f, n)
                    evacuates(v.tensor_tensor(z if q < KD else msg[m % 2], bank(branch, f, n)[:, 0:W3], msg[m % 2],
                                              ALU.mult), branch, f, n)
                    wait_evac(v, branch, f, n)
                    if q < KD:
                        v.sem_inc(z_done, 1)
                    else:
                        v.tensor_tensor(z, z, msg[m % 2], ALU.add).then_inc(z_done, 1)
                        v.wait_ge(z_done, m + 1)
                    m += 1
                if q + 1 < 2 * KD:
                    lo_piece(M0 + 2 * q + 3)
            def split(k, i, u1):
                v.wait_ge(w_hi_done[k], i * 2 + u1)
                v.tensor_tensor(w_lo[k], wraw[k], w_hi[k], ALU.subtract).then_inc(w_lo_done[k], 1)

            def split_tile(i):
                r = rows(i)
                for c in range(2):
                    wait_full(v, "h2", i, c)
                    g = vec[:, 8 + 4 * c:12 + 4 * c].unsqueeze(2).to_broadcast([P, 4, r])
                    src = bank("h2", i, c).rearrange("p (a b) -> p a b", a=4)[:, :, 0:r]
                    evacuates(v.tensor_tensor(h2t[c][:, :, 0:r], src, g, ALU.mult), "h2", i, c)
                for c in range(2):
                    at_ = (slice(None), slice(4 * c, 4 * c + 4), slice(i * P, i * P + r))
                    wait_evac(v, "h2", i, c)
                    v.wait_ge(h_hi_done, 2 * i + c + 1)
                    v.tensor_tensor(h_lo[at_], h2t[c][:, :, 0:r], h_hi[at_], ALU.subtract).then_inc(h_lo_done, 1)
                v.wait_ge(h_lo_done, 2 * i + 2)

            v.wait_ge(st_out, 32 * GH)
            for i in range(NT + 2):
                if i < NT:
                    r = rows(i)
                    v.wait_ge(r_landed[i % 2], 16 * (i // 2 + 1))
                    for s in range(2):
                        wait_full(v, "wo", i, s)
                        evacuates(v.tensor_tensor(x2[0:r, i, 512 * s:512 * s + 512], bank("wo", i, s)[0:r, :],
                                                  xr[i % 2][0:r, 512 * s:512 * s + 512], ALU.add), "wo", i, s)
                        wait_evac(v, "wo", i, s)
                        v.sem_inc(r_used, 1)
                if 1 <= i <= NT:
                    mean_tile(i - 1, y_sq, y_ms)
                    norm_tile(i - 1, x2[:, i - 1, :], h2[(i - 1) % 2], y_rt, y_h)
                if i >= NT:
                    split(i - NT, 0, 1)
                if i >= 2:
                    split_tile(i - 2)
            def add_down(i, half, j, c):
                wait_full(v, "dn", half, j, c, more=i * PAIR)
                row = x2[0:rows(j), j, 512 * c:512 * c + 512]
                evacuates(v.tensor_tensor(row, bank("dn", half, j, c)[0:rows(j), :], row, ALU.add), "dn", half, j, c)

            def ff_unit(i, half, last=False):
                before = ("dn", 1 - half, NT - 1, 1)
                wait_evac(v, *before, more=i * PAIR + (PAIR * (half - 1)))
                split(2, i, half + 1)
                for m in range(6):
                    f, n = m // 3, m % 3
                    v.wait_ge(f_sig, i * 12 + (6 * half + m + 1))
                    evacuates(v.tensor_tensor(ft, bank("fg", half, f, n)[:, 0:W3], fsig[m % 2], ALU.mult),
                              "fg", half, f, n)
                    wait_evac(v, "fg", half, f, n, more=i * PAIR)
                    wait_full(v, "fu", half, f, n, more=i * PAIR)
                    evacuates(v.tensor_tensor(ft, bank("fu", half, f, n)[:, 0:W3], ft, ALU.mult), "fu", half, f, n)
                    wait_evac(v, "fu", half, f, n, more=i * PAIR)
                    v.wait_ge(a_hi_done, i * 12 + (6 * half + m + 1))
                    cols = slice(n * W3, (n + 1) * W3)
                    v.tensor_tensor(a_lo[:, f, cols], ft, a_hi[:, f, cols], ALU.subtract).then_inc(a_lo_done, 1)
                    v.wait_ge(a_lo_done, i * 12 + (6 * half + m + 1))
                if not last:
                    for j in range(NT):
                        if j in (1, 3):
                            split(j // 2, i, half + 2)
                        for c in range(2):
                            add_down(i, half, j, c)

            with v.Fori(0, PAIRS) as i:
                ff_unit(i, 0)
                ff_unit(i, 1)
            ff_unit(PAIRS, 0, True)
            v.wait_ge(g_landed, 16)
            for i in range(NT + 1):
                if i < NT:
                    for c in range(2):
                        add_down(PAIRS, 0, i, c)
                    for c in range(2):
                        wait_evac(v, "dn", 0, i, c, more=PAIRS * PAIR)
                    v.sem_inc(x2_done, 1)
                if i >= 1:
                    r = rows(i - 1)
                    v.wait_ge(z_rt, i)
                    link(v.reciprocal(rstd[0:r, i - 1:i], rt[0:r, i - 1:i]))
                    if i >= 4:
                        v.wait_ge(z_out[(i - 1) % 3], 16 * ((i - 1) // 3))
                    v.scalar_tensor_tensor(yo[(i - 1) % 3][0:r, :], x2[0:r, i - 1, :], rstd[0:r, i - 1:i], gfb[0:r, :],
                                           ALU.mult, ALU.mult).then_inc(z_o, 1)
                if i < NT:
                    mean_tile(i, z_sq, z_ms)

        @block.gpsimd
        def _(g):
            g.memset(kw[:, NTP, :], 0.0).then_inc(zeroed, 1)
            g.memset(qiS, 0.0).then_inc(zeroed, 1)
            g.memset(scs, 0.0).then_inc(zeroed, 1)
            g.wait_ge(c_landed, 16 * N_CONST)
            for n in range(DB * NPG):
                pg = g.value_load(pagetab[0:1, n:n + 1], min_val=0, max_val=a["cache_kidx"].shape[1] - 1)
                src = a["cache_kidx"][0, bass.ds(pg, 1)].rearrange("a s d -> (a s) d")
                for e in range(2):
                    g.dma_start(kpg[:, n, e * IDM:(e + 1) * IDM], src).then_inc(pg_landed, 16)
            for h in range(DH):
                wait_evac(g, "nb", h)
                g.dma_start(scr[h].rearrange("(p c) -> p c", c=384)[:, 0:383], nbs[h % 2]).then_inc(nb_out[h % 2], 16)
            all_nb_out(g)
            for h in range(DH):
                src = scr[h][127:127 + P * 383].rearrange("(p c) -> p c", c=383)[:, 0:256]
                g.dma_start(nearb[:, h, :], src).then_inc(nb_in, 16)
            g.wait_ge(kn_done, 1)
            g.dma_start(o["kidx_p"].rearrange("(i p) d -> p i d", p=P), kn[:, 0:NTP, 0:IDM]).then_inc(ki_out, 16)
            g.dma_start(o["kidx_s"], kn[0:NS, NTP, 0:IDM]).then_inc(ki_out, 16)
            for k, b in enumerate(range(2, NTP)):
                g.wait_ge(sc_done, k + 1)
                d = SC[:, SCAT[b] + b * P:SCAT[b] + (b + 1) * P]
                g.affine_select(out=d, in_=d, compare_op=ALU.is_ge, fill=NEG, base=0, pattern=[[-1, P]],
                                channel_multiplier=1).then_inc(sc_diag, 1)
            for i in range(NT):
                wait_evac(g, "kt", i)
                dst = o["k_p"][i * P:(i + 1) * P, :] if i < NTP else o["k_s"]
                g.dma_start(dst, kst[i % 2][0:rows(i), :]).then_inc(kt_out[i % 2], 16)
            for i in range(NT):
                wait_evac(g, "vd", i)
            g.dma_start(o["v_p"].rearrange("(i p) d -> p i d", p=P), vd[:, 0:NTP, :]).then_inc(outs, 16)
            g.dma_start(o["v_s"], vd[0:NS, NTP, :]).then_inc(outs, 16)
            g.wait_ge(nb_in, 16 * DH)
            g.wait_ge(ki_out, 32)
            all_kt_out(g)
            g.memset(nearz, 0.0).then_inc(pool_seq, 1)
            g.wait_ge(pool_seq, 1)
            g.affine_select(out=nearz[:, P:], in_=nearz[:, P:], compare_op=ALU.is_ge, fill=NEG, base=0,
                            pattern=[[-1, P]], channel_multiplier=1).then_inc(pool_seq, 1)
            g.wait_ge(pool_seq, 2)
            for u, (b, h) in enumerate(UN):
                if u >= 4:
                    g.wait_ge(lg_used, u - 3)
                if b >= 2 and h == 0:
                    g.wait_ge(mask_done, b - 1)
                L = P * (b + 1)
                m = SC[:, SCAT[b] + L - 256:SCAT[b] + L] if b >= 2 else nearz
                g.tensor_tensor(nearm[u % 4], m, nearb[:, h, :], ALU.add).then_inc(near_done, 1)
            def page(b, p, names):
                n = b * NPG + p
                pg = g.value_load(pagetab[0:1, n:n + 1], min_val=0, max_val=a["cache_k"].shape[1] - 1)
                for name, dst, s_ in names:
                    g.dma_start(dst[:, p, :], a[name][0, bass.ds(pg, 1)].rearrange("a s h d -> (a s) (h d)"))\
                     .then_inc(s_, 16)

            g.wait_ge(lg_used, DH * (NTP - 1))
            for b in range(2):
                for p in range(NPG):
                    page(b, p, [("cache_k", kpS[b % 2], ks_landed[b % 2])])
            g.wait_ge(pr_done, len(UN))
            wait_full(g, "o", len(UN) - 1)
            wait_evac(g, "ot", NTP - 1)
            def values(b):
                for p in range(NPG):
                    page(b, p, [("cache_v", vpS[b], vs_landed[b // 4])])

            for b in range(4):
                values(b)
            for b in range(2, DB):
                wait_full(g, "kp", (b - 2) // 4, (b - 2) % 4, 1)
                for p in range(NPG):
                    page(b, p, [("cache_k", kpS[b % 2], ks_landed[b % 2])])
            values(4)
            values(5)
            wait_full(g, "so", 0)
            values(6)
            values(7)
            g.dma_start(wgu[0:RANK, :], a["w_gate_up"][0]).then_inc(wgu_in, 16)
            wait_evac(g, "sot", 0)
            wait_evac(g, "sot", 1)
            g.dma_start(od_mem, arena[:, o_odT:o_odT + 4 * T]).then_inc(od_out, 16)
            g.memset(rst, 1.0).then_inc(pool_seq, 1)
            g.wait_ge(pool_seq, 3)
            g.memset(rst[:, 0:SEQ].rearrange("p (c s) -> p c s", s=P)[:, :, 0:1], 0.0).then_inc(pool_seq, 1)
            g.memset(rst[:, SEQ:T].rearrange("p (c s) -> p c s", s=DT)[:, :, 0:1], 0.0).then_inc(zeroed, 1)
            for h in range(GH):
                if h >= 1:
                    g.wait_ge(st_out, 32 * h)
                g.dma_start(S0, a["state_gla"][0, :, h].rearrange("b k v -> k b v")).then_inc(st_in, 16)
                g.wait_ge(core_done, 2 * h + 1)
                g.dma_start(o["gla_p"][h], Sp).then_inc(st_out, 16)
                if h == GH - 1:
                    wait_full(g, "at", h, NTP)
                    g.dma_start(od_whole, od_mem.rearrange("p (k t) -> p k t", t=T)).then_inc(od_landed, 16)
                g.wait_ge(core_done, 2 * h + 2)
                g.dma_start(o["gla_s"][:, h].rearrange("b k v -> k b v"), S0).then_inc(st_out, 16)
                for i in range(NT):
                    wait_evac(g, "gt", h, i)
                g.dma_start(og_mem[:, 2 * h * T:2 * (h + 1) * T].rearrange("p (k t) -> p k t", t=T), ogs)\
                 .then_inc(og_out, 16)
            g.wait_ge(og_out, 16 * GH)
            for k in range(KD):
                g.wait_ge(p_lo_done, M0 + 3 + k)
                g.dma_start(og_whole[:, k, :], og_mem[:, k * T:(k + 1) * T]).then_inc(og_landed, 16)
            wait_full(g, "fu", 0, 1, 2, more=PAIRS * PAIR)
            wait_full(g, "fg", 0, 1, 2, more=PAIRS * PAIR)
            g.dma_start(gfb, a["g_final"].rearrange("(o n) -> o n", o=1).to_broadcast([P, D])).then_inc(g_landed, 16)
            for i in range(NT):
                g.wait_ge(z_o, i + 1)
                dst = o["y_p"][i * P:(i + 1) * P, :] if i < NTP else o["y_s"]
                g.dma_start(dst, yo[i % 3][0:rows(i), :]).then_inc(z_out[i % 3], 16)
            g.wait_ge(outs, 32)
            g.wait_ge(st_out, 32 * GH)
            all_kt_out(g)
            for k in range(3):
                g.wait_ge(z_out[k], 16 * 3)


def kernel(**inputs):
    import concourse.bacc as bacc
    from concourse.bass_utils import run_bass_kernel_spmd

    c128, c32, bits = constants()
    at128, _ = widths(c128)
    at32, _ = widths(c32)
    arrays = {k: np.ascontiguousarray(v) for k, v in inputs.items()}
    arrays["c128"] = np.concatenate(list(c128.values()), 1)
    arrays["c32"] = np.concatenate(list(c32.values()), 1)
    arrays["cbits"] = bits
    nc = bacc.Bacc("TRN2", target_bir_lowering=False, num_devices=1)
    a = {k: nc.dram_tensor(k, v.shape, mybir.dt.from_np(v.dtype), kind="ExternalInput").ap()
         for k, v in arrays.items()}
    shapes = {"y_p": [SEQ, D], "y_s": [NS, D], "k_p": [SEQ, DW], "v_p": [SEQ, DW], "kidx_p": [SEQ, IDM],
              "gla_p": [GH, GDK, GDV], "k_s": [NS, DW], "v_s": [NS, DW], "kidx_s": [NS, IDM],
              "gla_s": [DB, GH, GDK, GDV]}
    o = {k: nc.dram_tensor("out_" + k, s, F32, kind="ExternalOutput").ap() for k, s in shapes.items()}
    build(nc, a, o, at128, at32)
    r = run_bass_kernel_spmd(nc, [arrays], core_ids=[0]).results[0]
    g = {k: r["out_" + k] for k in shapes}
    return (g["y_p"].reshape(1, SEQ, D), g["y_s"].reshape(DB, DT, D),
            g["k_p"].reshape(1, 1, SEQ, DH, DHD), g["v_p"].reshape(1, 1, SEQ, DH, DHD),
            g["kidx_p"].reshape(1, 1, SEQ, IDM), g["gla_p"].reshape(1, 1, GH, GDK, GDV),
            g["k_s"].reshape(1, DB, DT, DH, DHD), g["v_s"].reshape(1, DB, DT, DH, DHD),
            g["kidx_s"].reshape(1, DB, DT, IDM), g["gla_s"].reshape(1, DB, GH, GDK, GDV))
```
